# Optimizing a Trainium2 kernel written in Bass

```python
import jax, jax.numpy as jnp
from jax import lax
import numpy as np

D_MODEL = 1024
BATCH = 1
SEQ = 256
DEPTH = 1

CHUNK = 64

SB_HEAD_DIM = 64
SB_HEADS = 4
SB_WIDTH = SB_HEADS * SB_HEAD_DIM
Q_BLOCK = 128
SUB = 32

POOL_WINDOWS = (2, 4, 8, 16)
POOL_GROUPS = len(POOL_WINDOWS)
POOL_WIDTH = D_MODEL - SB_WIDTH
POOL_GROUP_DIM = POOL_WIDTH // POOL_GROUPS

N_BRANCHES = 2
IN_WIDTH = 3 * SB_WIDTH + POOL_WIDTH + N_BRANCHES * D_MODEL

N_EXPERTS = 32
TOP_K = 4
D_EXPERT = D_MODEL
SWIGLU_LIMIT = 7.0
SWIGLU_ALPHA = 1.702
EXPERT_BLOCK = 256

NORM_EPS = 1e-6

kernel_name = "hybrid_stickbreak_pool_moe_encoder"

def rmsnorm(x, g):
    xf = x.astype(jnp.float32)
    r = lax.rsqrt(jnp.mean(xf * xf, axis=-1, keepdims=True) + NORM_EPS)
    return (xf * r * g.astype(jnp.float32)).astype(x.dtype)

def stick_breaking_attention(q, k, v):
    B, S, H, hd = q.shape
    qf = q.astype(jnp.float32) * (1.0 / np.sqrt(hd).astype(np.float32))
    kf = k.astype(jnp.float32)
    vf = v.astype(jnp.float32)
    tri_incl = jnp.tri(SUB, dtype=jnp.float32)
    outs = []
    for i in range(S // Q_BLOCK):
        n_k = (i + 1) * Q_BLOCK
        n_sub = n_k // SUB
        qb = qf[:, i * Q_BLOCK:(i + 1) * Q_BLOCK]
        kb = kf[:, :n_k]
        vb = vf[:, :n_k]
        z = jnp.einsum('bqhd,bkhd->bhqk', qb, kb)
        qpos = i * Q_BLOCK + jnp.arange(Q_BLOCK)
        mask = jnp.arange(n_k)[None, :] < qpos[:, None]
        log_keep = jnp.where(mask, jax.nn.log_sigmoid(-z), 0.0)
        lr = log_keep.reshape(B, H, Q_BLOCK, n_sub, SUB)
        r_in = jnp.einsum('bhqnj,jk->bhqnk', lr, tri_incl)
        after = jnp.einsum('bhqn,nm->bhqm', lr.sum(-1), jnp.tri(n_sub, k=-1, dtype=jnp.float32))
        log_a = z + (r_in + after[..., None]).reshape(B, H, Q_BLOCK, n_k)
        a = jnp.exp(jnp.where(mask, log_a, -jnp.inf))
        outs.append(jnp.einsum('bhqk,bkhd->bqhd', a, vb))
    o = jnp.concatenate(outs, axis=1)
    return o.reshape(B, S, H * hd)

def multi_scale_pool(u, pool_w, pool_b, pool_scale):
    B, S, G, Cg = u.shape
    uf = u.astype(jnp.float32)
    cs0 = jnp.concatenate([jnp.zeros((B, 1, G, Cg), jnp.float32), jnp.cumsum(uf, axis=1)], axis=1)
    t1 = jnp.arange(1, S + 1).astype(jnp.float32)
    outs = []
    for g, w in enumerate(POOL_WINDOWS):
        cg = cs0[:, :, g]
        lo = jnp.pad(cg[:, :S - w + 1], ((0, 0), (w - 1, 0), (0, 0)))
        mean = (cg[:, 1:] - lo) / jnp.minimum(t1, float(w))[None, :, None]
        outs.append(mean - uf[:, :, g])
    mixed = jnp.stack(outs, axis=2)
    y = jnp.einsum('bsgc,gcd->bsgd', mixed, pool_w.astype(jnp.float32)) + pool_b.astype(jnp.float32)
    y = y * pool_scale.astype(jnp.float32)
    return y.reshape(B, S, G * Cg)

def hybrid_mixer(h, w_in, pool_w, pool_b, pool_scale, w_br_attn, w_br_pool, w_out):
    B, S, _ = h.shape
    p = h @ w_in
    q, k, v, u, g = jnp.split(p, [SB_WIDTH, 2 * SB_WIDTH, 3 * SB_WIDTH, 3 * SB_WIDTH + POOL_WIDTH], axis=-1)
    shp = (B, S, SB_HEADS, SB_HEAD_DIM)
    attn = stick_breaking_attention(q.reshape(shp), k.reshape(shp), v.reshape(shp)).astype(h.dtype)
    pool = multi_scale_pool(u.reshape(B, S, POOL_GROUPS, POOL_GROUP_DIM), pool_w, pool_b, pool_scale).astype(h.dtype)
    g_attn, g_pool = jnp.split(jax.nn.sigmoid(g), N_BRANCHES, axis=-1)
    merged = g_attn * (attn @ w_br_attn) + g_pool * (pool @ w_br_pool)
    return merged @ w_out

def moe(h, router_w, router_b, w_gu, b_gu, w_dn, b_dn):
    B, S, D = h.shape
    T = B * S
    xt = h.reshape(T, D)
    logits = (xt @ router_w + router_b).astype(jnp.float32)
    top_v, top_i = lax.top_k(logits, TOP_K)
    gates = jax.nn.softmax(top_v, axis=-1)
    e_flat = top_i.reshape(-1)
    g_flat = gates.reshape(-1)
    tok_flat = jnp.repeat(jnp.arange(T, dtype=jnp.int32), TOP_K)
    order = jnp.argsort(e_flat)
    e_sorted = e_flat[order]
    counts = jnp.bincount(e_flat, length=N_EXPERTS)
    padded = ((counts + EXPERT_BLOCK - 1) // EXPERT_BLOCK) * EXPERT_BLOCK
    start = jnp.cumsum(counts) - counts
    pend = jnp.cumsum(padded)
    pstart = pend - padded
    rank = jnp.arange(T * TOP_K) - start[e_sorted]
    dest = pstart[e_sorted] + rank
    n_rows = T * TOP_K + N_EXPERTS * EXPERT_BLOCK
    n_blocks = n_rows // EXPERT_BLOCK
    row_tok = jnp.zeros((n_rows,), jnp.int32).at[dest].set(tok_flat[order])
    row_gate = jnp.zeros((n_rows,), jnp.float32).at[dest].set(g_flat[order])
    block_e = jnp.minimum(jnp.searchsorted(pend, jnp.arange(n_blocks) * EXPERT_BLOCK, side='right'), N_EXPERTS - 1)
    xr = xt[row_tok].reshape(n_blocks, EXPERT_BLOCK, D)

    def expert_block(args):
        xb, e = args
        gu = xb @ w_gu[e] + b_gu[e]
        gate, up = jnp.split(gu, 2, axis=-1)
        gate = jnp.minimum(gate, SWIGLU_LIMIT)
        up = jnp.clip(up, -SWIGLU_LIMIT, SWIGLU_LIMIT)
        act = (up + 1.0) * gate * jax.nn.sigmoid(SWIGLU_ALPHA * gate)
        return act @ w_dn[e] + b_dn[e]

    yr = lax.map(expert_block, (xr, block_e)).reshape(n_rows, D)
    y = jax.ops.segment_sum(yr.astype(jnp.float32) * row_gate[:, None], row_tok, num_segments=T)
    return y.reshape(B, S, D).astype(h.dtype)

def setup_inputs(seed: int = 0) -> dict:
    key = jax.random.key(seed)
    ks = jax.random.split(key, 24)
    L, D = DEPTH, D_MODEL

    def nrm(k, shape, scale):
        return jax.random.normal(k, shape, jnp.float32) * scale

    return {
        "x": nrm(ks[0], (BATCH, SEQ, D), 1.0),
        "c": nrm(ks[1], (BATCH, D), 1.0),
        "ada_w": nrm(ks[2], (L, D, 6 * D), 0.5 * D ** -0.5),
        "ada_b": nrm(ks[3], (L, 6 * D), 0.01),
        "pre1_g": 1.0 + nrm(ks[4], (L, D), 0.05),
        "post1_g": 1.0 + nrm(ks[5], (L, D), 0.05),
        "pre2_g": 1.0 + nrm(ks[6], (L, D), 0.05),
        "post2_g": 1.0 + nrm(ks[7], (L, D), 0.05),
        "w_in": nrm(ks[8], (L, D, IN_WIDTH), D ** -0.5),
        "pool_w": nrm(ks[9], (L, POOL_GROUPS, POOL_GROUP_DIM, POOL_GROUP_DIM), POOL_GROUP_DIM ** -0.5),
        "pool_b": nrm(ks[10], (L, POOL_GROUPS, POOL_GROUP_DIM), 0.01),
        "pool_scale": 1.0 + nrm(ks[11], (L, POOL_GROUPS, POOL_GROUP_DIM), 0.1),
        "w_br_attn": nrm(ks[12], (L, SB_WIDTH, D), SB_WIDTH ** -0.5),
        "w_br_pool": nrm(ks[13], (L, POOL_WIDTH, D), POOL_WIDTH ** -0.5),
        "w_out": nrm(ks[14], (L, D, D), D ** -0.5),
        "router_w": nrm(ks[15], (L, D, N_EXPERTS), D ** -0.5),
        "router_b": nrm(ks[16], (L, N_EXPERTS), 0.01),
        "w_gu": nrm(ks[17], (L, N_EXPERTS, D, 2 * D_EXPERT), D ** -0.5),
        "b_gu": nrm(ks[18], (L, N_EXPERTS, 2 * D_EXPERT), 0.01),
        "w_dn": nrm(ks[19], (L, N_EXPERTS, D_EXPERT, D), D_EXPERT ** -0.5),
        "b_dn": nrm(ks[20], (L, N_EXPERTS, D), 0.01),
    }

def reference(x, c, ada_w, ada_b, pre1_g, post1_g, pre2_g, post2_g, w_in, pool_w, pool_b, pool_scale,
              w_br_attn, w_br_pool, w_out, router_w, router_b, w_gu, b_gu, w_dn, b_dn):
    c_act = jax.nn.silu(c)
    for l in range(DEPTH):
        mod = (c_act @ ada_w[l] + ada_b[l])[:, None, :]
        shift1, scale1, gate1, shift2, scale2, gate2 = jnp.split(mod, 6, axis=-1)
        h = rmsnorm(x, pre1_g[l]) * (1.0 + scale1) + shift1
        y = hybrid_mixer(h, w_in[l], pool_w[l], pool_b[l], pool_scale[l], w_br_attn[l], w_br_pool[l], w_out[l])
        x = x + gate1 * rmsnorm(y, post1_g[l])
        h = rmsnorm(x, pre2_g[l]) * (1.0 + scale2) + shift2
        y = moe(h, router_w[l], router_b[l], w_gu[l], b_gu[l], w_dn[l], b_dn[l])
        x = x + gate2 * rmsnorm(y, post2_g[l])
    return x


_drawn_inputs = setup_inputs


def setup_inputs(seed=0):
    import zlib

    import numpy as np

    out = dict(_drawn_inputs(seed))
    spreads = {}
    factors = {'post2_g': 4.141, 'pool_b': 2.732, 'b_gu': 8.0, 'b_dn': 8.0}
    for name, (base, spread) in spreads.items():
        noise = np.random.default_rng([zlib.crc32(name.encode()), seed]).standard_normal(out[name].shape)
        drawn = base * np.exp(spread * noise) if base else spread * noise
        out[name] = __import__('jax').numpy.asarray(drawn.astype(out[name].dtype))
    for name, factor in factors.items():
        out[name] = (out[name] * factor).astype(out[name].dtype)
    return out
```

```python
import concourse.bass as bass
from concourse import mybir
from contextlib import ExitStack

P = 128
SEQ, D = 256, 1024
TT = SEQ // P
DB = D // P
BANK = 512
HEADS, HD = 4, 64
ATTN_W = HEADS * HD
POOL_W = D - ATTN_W
WINDOWS = (2, 4, 8, 16)
GROUP = POOL_W // len(WINDOWS)
PB = POOL_W // P
IN_W = 3 * ATTN_W + POOL_W + 2 * D
EXPERTS, TOP_K = 32, 4
F = D
CAP = 64
CHUNKS = SEQ // CAP
MAX_CHUNKS = EXPERTS + SEQ * TOP_K // CAP
LIMIT, ALPHA, EPS = 7.0, 1.702, 1e-6

CONSTS = {}
_at = 0
for _name, _width in (("ident", P), ("tri_neg", P), ("ones_neg", P), ("before", P), ("ones", P),
                      ("band0", len(WINDOWS) * SEQ), ("band1", len(WINDOWS) * P),
                      ("slot", CHUNKS * P), ("expert", EXPERTS), ("before_e", EXPERTS + 1), ("quad", 4)):
    CONSTS[_name] = (_at, _at + _width)
    _at += _width
CONST_W = _at

ROWS = {}
_at = 0
for _name, _count in (("ada_b", 6 * DB), ("pre1_g", DB), ("post1_g", DB), ("pre2_g", DB),
                      ("post2_g", DB), ("c", DB), ("pool_b", PB), ("pool_scale", PB)):
    ROWS[_name] = (_at, _at + _count)
    _at += _count
N_ROWS = _at

SLOTS, SLOT_W = 12, 2048
MIX_UNITS = ([("ada0", k) for k in range(DB)] + [("w_in", i) for i in range(2 * IN_W // BANK)]
             + [("br_attn", 0)] + [("br_pool", i) for i in range(3)]
             + [("ada1", k) for k in range(DB)] + [("w_out", i) for i in range(4)]
             + [("ada2", k) for k in range(DB)])
N_MIX = len(MIX_UNITS)
GU_UNITS, DN_UNITS = DB, 4
assert GU_UNITS + DN_UNITS == SLOTS


def unit_of(name, i):
    return MIX_UNITS.index((name, i))


def build(nc, x, c, ada_w, ada_b, pre1_g, post1_g, pre2_g, post2_g, w_in, pool_w, pool_b, pool_scale,
          w_br_attn, w_br_pool, w_out, router_w, router_b, w_gu, b_gu, w_dn, b_dn, consts, out):
    f32, i32, u32 = mybir.dt.float32, mybir.dt.int32, mybir.dt.uint32
    ALU = mybir.AluOpType
    ACT = mybir.ActivationFunctionType
    AX = mybir.AxisListType

    ctx = ExitStack()
    with ctx:
        def sb(name, shape, dt=f32):
            return ctx.enter_context(nc.sbuf_tensor(name, shape, dt))

        def sem(name):
            return ctx.enter_context(nc.semaphore(name))

        ring = sb("ring", [P, SLOTS, SLOT_W])
        const = sb("const", [P, CONST_W])
        rows = sb("rows", [N_ROWS, P])
        cols = sb("cols", [P, N_ROWS])
        x_sb = sb("x_sb", [P, TT, D])
        hT = sb("hT", [P, DB, SEQ])
        vu = sb("vu", [P, TT, D])
        merged = sb("merged", [P, TT, D])
        area = sb("area", [P, 4096])
        area2 = sb("area2", [P, 3 * 1536])
        qkT = sb("qkT", [P, 4, SEQ])
        attnT = sb("attnT", [P, 2, SEQ])
        poolw_sb = sb("poolw_sb", [P, PB, GROUP])
        spread = sb("spread", [P, D])
        bgu_sb = sb("bgu_sb", [EXPERTS, 2 * F])
        bdn_sb = sb("bdn_sb", [EXPERTS, D])
        rw_sb = sb("rw_sb", [P, DB, EXPERTS])
        rb_sb = sb("rb_sb", [1, EXPERTS])
        modrow = sb("modrow", [P, BANK])
        mod = sb("mod", [P, 6 * DB])
        fac = sb("fac", [P, 4, DB])
        csig = sb("csig", [P, DB])
        cact = sb("cact", [P, DB, 32])
        stat = sb("stat", [P, 16])
        top_v = sb("top_v", [P, TT, 8])
        top_i = sb("top_i", [P, TT, 8], u32)
        top_f = sb("top_f", [P, TT, TOP_K])
        top_e = sb("top_e", [P, TT, TOP_K])
        top_g = sb("top_g", [P, TT, TOP_K])
        logit = sb("logit", [P, TT, EXPERTS])
        mask = sb("mask", [P, TT, EXPERTS])
        gate = sb("gate", [P, TT, EXPERTS])
        rank = sb("rank", [P, TT, EXPERTS])
        gateT = sb("gateT", [EXPERTS, SEQ])
        nchunk = sb("nchunk", [EXPERTS, 4])
        base = sb("base", [1, 2 * EXPERTS + 1], i32)
        esel = sb("esel", [EXPERTS, CAP])

        def k(name):
            a, b = CONSTS[name]
            return const[:, a:b]

        def col(name, a=0, b=None):
            lo, hi = ROWS[name]
            return cols[:, lo + a:(lo + b if b is not None else hi)]

        ident, ones = k("ident"), k("ones")
        band0 = k("band0").rearrange("p (g t) -> p g t", t=SEQ)
        band1 = k("band1").rearrange("p (g t) -> p g t", t=P)
        slot = k("slot").rearrange("p (c s) -> p c s", s=P)
        gates = area[:, :].rearrange("p (t n) -> p t n", t=TT)
        xhat = merged
        sp0 = area2[:, 0:1024].rearrange("p (a b q) -> p a b q", a=2, b=2)
        sp1 = area2[:, 1024:1536].rearrange("p (a b q) -> p a b q", a=2, b=2)
        e0, e1 = area2[:, 1536:2560], area2[:, 2560:3072]
        a0 = area2[:, 3072:4096].rearrange("p (a b q) -> p a b q", a=2, b=2)
        a1 = area2[:, 4096:4608].rearrange("p (a b q) -> p a b q", a=2, b=2)
        mixT = area2[:, 0:1536].rearrange("p (b t) -> p b t", t=SEQ)
        poolT = area2[:, 1536:3072].rearrange("p (b t) -> p b t", t=SEQ)
        prod = area2[:, 3072:3072 + 1024].rearrange("p (a n) -> p a n", a=2)
        diag = area2[:, 0:1024].rearrange("p (b n) -> p b n", n=P)
        junk = area2[:, 0:1024]
        tail = area2[:, 1024:3072].rearrange("p (t n) -> p t n", t=TT)
        xn2, yacc = vu, merged
        hot = area[:, 0:256].rearrange("p (t r e) -> p t r e", t=TT, r=TOP_K)
        hotg = area[:, 256:512].rearrange("p (t r e) -> p t r e", t=TT, r=TOP_K)
        pick = area[:, 0:128].rearrange("p (t s) -> p t s", t=TT)
        pickg = area[:, 128:384].rearrange("p (t s) -> p t s", t=TT)
        xg = area[:, 384:896].rearrange("p (b s) -> p b s", s=CAP)
        xg_m = area[:, 896:1408].rearrange("p (b s) -> p b s", s=CAP)
        g_min, g_sig = area[:, 1408:1920], area[:, 1920:2432]
        u_clip, g_act, act_sb = area[:, 2432:2944], area[:, 2944:3456], area[:, 3456:3968]
        actT = area2[:, 3072:3584].rearrange("p (j s) -> p j s", s=P)
        ye = area2[:, 3584:4096]
        pickT = area2[:, 4096:4352]

        ps = ctx.enter_context(nc.psum_tensor("ps", [P, 8, BANK], f32))
        xT_ps = ps[:, 0:4, :].rearrange("p k (b t) -> p (k b) t", t=SEQ)
        GATE, UP, GATHER, DOWN, TURN = range(5)

        const_in, rows_in, x_in, poolw_in, router_in, bias_in = map(
            sem, ("const_in", "rows_in", "x_in", "poolw_in", "router_in", "bias_in"))
        unit_in = [sem(f"unit_in{i}") for i in range(SLOTS)]
        unit_used = sem("unit_used")
        names = ("rows_turned", "cols_ready", "csig_ready", "cact_ready", "squares_ready", "var_ready",
                 "std_ready", "rstd_ready", "xhat_ready", "x_turned", "modrow_ready",
                 "modcol_done", "mod_ready", "hT_ready", "q_done", "qk_ready", "in_done", "vu_ready",
                 "gates_ready", "z_done", "sp_part", "sp_ready", "sp_masked", "loga_done", "a_ready",
                 "a_masked", "o_done", "attnT_ready", "mix_done", "mixT_ready", "pool_done", "even_done",
                 "poolT_ready", "brA_done", "brA_ready", "brP_done", "brP_ready", "m_turned",
                 "mT_ready", "diag_ready", "spread_done", "spread_ready", "x1_ready",
                 "xn2_ready", "x2_turned", "h2_ready", "logit_done", "logit_ready", "exp_ready",
                 "mask_ready", "gate_ready", "rank_done", "count_done", "nchunk_ready", "base_done",
                 "base_ready", "gateT_done", "gateT_ready", "bias_done", "dve_step",
                 "act_step", "out_done", "rank_ready")
        s = {n: sem(n) for n in names}
        names = ("pick_ready", "gathered", "xgm_ready", "xg_ready", "gu_done", "gmin_ready", "sig_ready",
                 "u_ready", "gact_ready", "act_ready", "turned", "actT_ready", "down_done", "ye_ready",
                 "pick_turned", "pickT_ready", "scattered", "acc_ready")
        m = {n: sem(n) for n in names}
        block = ctx.enter_context(nc.Block())

        def slot_of(u):
            return ring[:, u % SLOTS, :]

        def ge(engine, semaphore, value):
            if isinstance(value, int) and value <= 0:
                return
            engine.wait_ge(semaphore, value)

        def expert_units(first, count, e):
            for j in range(first, first + count):
                u = N_MIX + j
                yield u % SLOTS, 16 * (u // SLOTS + 1) + 16 * e

        def used(engine, name, i):
            engine.wait_ge(unit_used, unit_of(name, i) + 1)

        def in_block_done(engine, n, t):
            if t == 0:
                engine.wait_ge(s["in_done"], n)
            else:
                used(engine, "w_in", 2 * n + 1)

        def branch_done(engine, semaphore, name, i, t, h):
            if (t, h) != (1, 1):
                engine.wait_ge(semaphore, 2 * t + h + 1)
            else:
                used(engine, name, i)

        @block.sync
        def _(sp):
            sp.dma_start(const[:, :], consts).then_inc(const_in, 16)
            sp.dma_start(x_sb[:, :, :], x[0].rearrange("(t p) n -> p t n", p=P)).then_inc(x_in, 16)
            ada_v = ada_w[0].rearrange("(k p) n -> p k n", p=P)
            win_v = w_in[0].rearrange("(k p) n -> p k n", p=P)
            for u, (name, i) in enumerate(MIX_UNITS):
                dst = slot_of(u)
                if name.startswith("ada"):
                    j = int(name[3])
                    src = ada_v[:, i, j * 2 * D:(j + 1) * 2 * D]
                elif name == "w_in":
                    n, half = i // 2, i % 2
                    dst = dst.rearrange("p (k n) -> p k n", n=BANK)
                    src = win_v[:, 4 * half:4 * half + 4, n * BANK:(n + 1) * BANK]
                else:
                    w = {"br_attn": w_br_attn, "br_pool": w_br_pool, "w_out": w_out}[name]
                    dst = dst.rearrange("p (k n) -> p k n", n=D)
                    src = w[0].rearrange("(k p) n -> p k n", p=P)[:, 2 * i:2 * i + 2, :]
                ge(sp, unit_used, u - SLOTS + 1)
                sp.dma_start(dst, src).then_inc(unit_in[u % SLOTS], 16)

            def expert(e, gu_free, dn_free):
                for j in range(SLOTS):
                    u = N_MIX + j
                    if j < GU_UNITS:
                        dst, src = slot_of(u), w_gu[0, e, j * P:(j + 1) * P, :]
                        gu_free(j)
                    else:
                        i = j - GU_UNITS
                        dst = slot_of(u).rearrange("p (k n) -> p k n", n=D)
                        src = w_dn[0, e, 2 * i * P:2 * (i + 1) * P, :].rearrange("(k p) n -> p k n", p=P)
                        dn_free(j)
                    sp.dma_start(dst, src).then_inc(unit_in[u % SLOTS], 16)

            def mixer_used(j):
                ge(sp, unit_used, N_MIX + j - SLOTS + 1)

            expert(0, mixer_used, mixer_used)
            sp.wait_ge(s["base_ready"], 1)
            with sp.Fori(1, EXPERTS) as e:
                b0 = sp.value_load(base[0:1, bass.ds(e, 1)], min_val=1, max_val=MAX_CHUNKS)

                def gu_free(j):
                    if j == 0:
                        sp.wait_ge(m["gu_done"], b0)

                def dn_free(j):
                    if j == GU_UNITS:
                        sp.wait_ge(m["down_done"], b0)

                expert(e, gu_free, dn_free)
            for t in range(TT):
                sp.wait_ge(s["out_done"], t + 1)
                sp.dma_start(out[0, t * P:(t + 1) * P, :], tail[:, t, :]).then_inc(x_in, 16)
            sp.wait_ge(x_in, 16 * (1 + TT))

        @block.tensor
        def _(pe):
            mm = nc.tensor.matmul

            def arrived(u):
                pe.wait_ge(unit_in[u % SLOTS], 16 * (u // SLOTS + 1))

            def ada_rows(j, bank):
                for kk in range(DB):
                    u = unit_of(f"ada{j}", kk)
                    arrived(u)
                    for q in range(4):
                        last = mm(ps[32 * q:32 * q + 32, bank, :], cact[:, kk, :],
                                  slot_of(u)[:, q * BANK:(q + 1) * BANK], start=(kk == 0), stop=(kk == DB - 1))
                    last.then_inc(unit_used, 1)

            def ada_cols(j, bank):
                pe.wait_ge(s["modrow_ready"], j + 1)
                view = ps[:, bank, 0:16].rearrange("p (q i) -> p i q", i=4)
                for i in range(4):
                    last = mm(view[:, i, :], modrow[:, i * P:(i + 1) * P], k("quad"), start=True, stop=True)
                last.then_inc(s["modcol_done"], 1)

            def spread_over(n, bank):
                pe.wait_ge(s["diag_ready"], n)
                for h in range(2):
                    last = mm(ps[:, bank + h, :], ones, diag[:, 4 * h:4 * h + 4, :], start=True, stop=True)
                last.then_inc(s["spread_done"], 1)

            pe.wait_ge(const_in, 16)
            pe.wait_ge(rows_in, 16 * len(ROWS))
            nc.tensor.transpose(ps[:, 5, 0:N_ROWS], rows[:, :], ident[0:N_ROWS, 0:N_ROWS])\
                .then_inc(s["rows_turned"], 1)
            for t in range(TT):
                pe.wait_ge(s["xhat_ready"], t + 1)
                for b in range(DB):
                    last = nc.tensor.transpose(xT_ps[:, b, t * P:(t + 1) * P], xhat[:, t, b * P:(b + 1) * P], ident)
            last.then_inc(s["x_turned"], 1)
            pe.wait_ge(s["cact_ready"], 1)
            ada_rows(0, 4)
            pe.wait_ge(s["cols_ready"], 1)
            ada_cols(0, 5)

            pe.wait_ge(s["hT_ready"], 2)
            for n in range(2):
                arrived(unit_of("w_in", n))
            for fb in range(4):
                for kk in range(DB):
                    u = unit_of("w_in", kk // 4)
                    w = slot_of(u).rearrange("p (k n) -> p k n", n=BANK)
                    last = mm(ps[:, 6 + fb // 2, (fb % 2) * SEQ:(fb % 2 + 1) * SEQ],
                              w[:, kk % 4, fb * P:(fb + 1) * P], hT[:, kk, :], start=(kk == 0), stop=(kk == DB - 1))
                if fb == 1:
                    last.then_inc(s["q_done"], 1)
            last.then_inc(unit_used, 2)

            def in_block(n):
                for t in range(TT):
                    for kk in range(DB):
                        u = unit_of("w_in", 2 * n + kk // 4)
                        arrived(u)
                        w = slot_of(u).rearrange("p (k n) -> p k n", n=BANK)
                        last = mm(ps[:, 2 * ((n - 1) % 2) + t, :], hT[:, kk, t * P:(t + 1) * P], w[:, kk % 4, :],
                                  start=(kk == 0), stop=(kk == DB - 1))
                    if t == 0:
                        last.then_inc(s["in_done"], 1)
                last.then_inc(unit_used, 2)

            in_block(1)
            in_block(2)

            def z_into(first):
                for head in range(HEADS):
                    par, b = head % 2, head // 2
                    q, kT = qkT[par * HD:par * HD + HD, b, :], qkT[par * HD:par * HD + HD, 2 + b, :]
                    mm(ps[:, 4 + par, b * SEQ:(b + 1) * SEQ], kT[:, 0:P], q, start=first, stop=True,
                       skip_group_check=not first)
                    last = mm(ps[:, 6 + par, b * P:(b + 1) * P], kT[:, P:SEQ], q[:, P:SEQ], start=first, stop=True,
                              skip_group_check=not first)
                return last

            pe.wait_ge(s["qk_ready"], 2)
            z_into(True).then_inc(s["z_done"], 1)
            pe.wait_ge(s["vu_ready"], 2)
            in_block(3)
            pe.wait_ge(s["vu_ready"], 4)
            in_block(4)
            pe.wait_ge(s["sp_masked"], 2)
            for par in range(2):
                mm(ps[:, 4 + par, :], k("tri_neg"), sp0[:, par], start=True, stop=True)
                mm(ps[:, 4 + par, :].rearrange("p (b q) -> p b q", b=2)[:, :, P:SEQ], k("ones_neg"), sp1[:, par],
                   start=False, stop=True, skip_group_check=True)
                mm(ps[:, 6 + par, 0:SEQ], k("tri_neg"), sp1[:, par], start=True, stop=True)
            z_into(False).then_inc(s["loga_done"], 1)
            pe.wait_ge(s["gates_ready"], 2)
            in_block(5)
            pe.wait_ge(s["a_masked"], 2)
            for head in range(HEADS):
                par, b = head % 2, head // 2
                o = ps[par * HD:par * HD + HD, 4, b * SEQ:(b + 1) * SEQ]
                mm(o, vu[:, 0, head * HD:(head + 1) * HD], a0[:, par, b, :], start=True, stop=True)
                last = mm(o[:, P:SEQ], vu[:, 1, head * HD:(head + 1) * HD], a1[:, par, b, :], start=False, stop=True,
                          skip_group_check=True)
            last.then_inc(s["o_done"], 1)
            for b in range(PB):
                for g in range(len(WINDOWS)):
                    lo, hi = max(b * P, g * GROUP), min((b + 1) * P, (g + 1) * GROUP)
                    if lo >= hi:
                        continue
                    o = ps[lo - b * P:hi - b * P, 5 + b // 2, (b % 2) * SEQ:(b % 2 + 1) * SEQ]
                    mm(o, vu[:, 0, ATTN_W + lo:ATTN_W + hi], band0[:, g, :], start=True, stop=True)
                    last = mm(o[:, P:SEQ], vu[:, 1, ATTN_W + lo:ATTN_W + hi], band1[:, g, :], start=False, stop=True,
                              skip_group_check=True)
            last.then_inc(s["mix_done"], 1)
            pe.wait_ge(s["gates_ready"], 4)
            in_block(6)
            pe.wait_ge(poolw_in, 16)
            pe.wait_ge(s["mixT_ready"], 1)

            def parts(g):
                found = []
                for b in range(PB):
                    lo, hi = max(b * P, g * GROUP), min((b + 1) * P, (g + 1) * GROUP)
                    if lo < hi:
                        found.append((b, lo - b * P, hi - b * P))
                return sorted(found, key=lambda f: f[2] - f[1])

            for g in (0, 2, 1, 3):
                if g == 1:
                    pe.wait_ge(s["even_done"], 1)
                for ob, olo, ohi in parts(g):
                    d0 = ob * P + olo - g * GROUP
                    ins = parts(g)
                    for n, (ib, ilo, ihi) in enumerate(ins):
                        last = mm(ps[olo:ohi, 5 + ob // 2, (ob % 2) * SEQ:(ob % 2 + 1) * SEQ],
                                  poolw_sb[ilo:ihi, ib, d0:d0 + ohi - olo], mixT[ilo:ihi, ib, :],
                                  start=(n == 0), stop=(n == len(ins) - 1))
                if g == 2:
                    last.then_inc(s["even_done"], 1)
            last.then_inc(s["pool_done"], 1)
            pe.wait_ge(s["gates_ready"], 8)
            pe.wait_ge(s["attnT_ready"], 1)
            arrived(unit_of("br_attn", 0))
            w = slot_of(unit_of("br_attn", 0)).rearrange("p (k n) -> p k n", n=D)
            for t in range(TT):
                for h in range(2):
                    for b in range(2):
                        last = mm(ps[:, 2 * t + h, :], attnT[:, b, t * P:(t + 1) * P],
                                  w[:, b, h * BANK:(h + 1) * BANK], start=(b == 0), stop=(b == 1))
                    if (t, h) != (1, 1):
                        last.then_inc(s["brA_done"], 1)
            last.then_inc(unit_used, 1)
            pe.wait_ge(s["poolT_ready"], 1)
            for i in range(3):
                arrived(unit_of("br_pool", i))
            for t in range(TT):
                for h in range(2):
                    for b in range(PB):
                        w = slot_of(unit_of("br_pool", b // 2)).rearrange("p (k n) -> p k n", n=D)
                        last = mm(ps[:, 4 + 2 * t + h, :], poolT[:, b, t * P:(t + 1) * P],
                                  w[:, b % 2, h * BANK:(h + 1) * BANK], start=(b == 0), stop=(b == PB - 1))
                    if (t, h) != (1, 1):
                        last.then_inc(s["brP_done"], 1)
            last.then_inc(unit_used, 3)
            pe.wait_ge(s["brA_ready"], 4)
            ada_rows(1, 0)
            pe.wait_ge(s["brP_ready"], 4)
            mT_ps = ps[:, 4:8, :].rearrange("p k (b t) -> p (k b) t", t=SEQ)
            for b in range(DB):
                for t in range(TT):
                    last = nc.tensor.transpose(mT_ps[:, b, t * P:(t + 1) * P], merged[:, t, b * P:(b + 1) * P], ident)
            last.then_inc(s["m_turned"], 1)
            pe.wait_ge(s["mT_ready"], 2)
            ada_cols(1, 4)
            for i in range(4):
                u = unit_of("w_out", i)
                arrived(u)
                w = slot_of(u).rearrange("p (k n) -> p k n", n=D)
                for kk in (2 * i, 2 * i + 1):
                    for t in range(TT):
                        for h in range(2):
                            last = mm(ps[:, 2 * t + h, :], hT[:, kk, t * P:(t + 1) * P],
                                      w[:, kk % 2, h * BANK:(h + 1) * BANK], start=(kk == 0), stop=(kk == DB - 1))
                last.then_inc(unit_used, 1)
            spread_over(1, 6)
            ada_rows(2, 5)
            pe.wait_ge(s["mod_ready"], 2)
            ada_cols(2, 4)
            pe.wait_ge(s["x1_ready"], 1)
            for t in range(TT):
                pe.wait_ge(s["xn2_ready"], t + 1)
                for b in range(DB):
                    last = nc.tensor.transpose(xT_ps[:, b, t * P:(t + 1) * P], xn2[:, t, b * P:(b + 1) * P], ident)
            last.then_inc(s["x2_turned"], 1)
            pe.wait_ge(s["h2_ready"], 2)
            pe.wait_ge(router_in, 32)
            for t in range(TT):
                o = ps[:, 5, t * EXPERTS:(t + 1) * EXPERTS]
                for kk in range(DB):
                    mm(o, hT[:, kk, t * P:(t + 1) * P], rw_sb[:, kk, :], start=(kk == 0), stop=False)
                last = mm(o, ones[0:1, :], rb_sb[0:1, :], start=False, stop=True)
            last.then_inc(s["logit_done"], 1)
            pe.wait_ge(s["mask_ready"], 1)
            for t in range(TT):
                last = mm(ps[0:EXPERTS, 4, 0:1], mask[:, t, :], ones[:, 0:1], start=(t == 0), stop=(t == 1))
            last.then_inc(s["count_done"], 1)
            mm(ps[:, 7, 0:EXPERTS], k("before"), mask[:, 0, :], start=True, stop=True)
            mm(ps[:, 7, EXPERTS:2 * EXPERTS], k("before"), mask[:, 1, :], start=True, stop=False)
            mm(ps[:, 7, EXPERTS:2 * EXPERTS], ones, mask[:, 0, :], start=False, stop=True)\
                .then_inc(s["rank_done"], 1)
            pe.wait_ge(s["gate_ready"], 1)
            for t in range(TT):
                last = nc.tensor.transpose(ps[0:EXPERTS, 6, t * P:(t + 1) * P], gate[:, t, :], ident)
            last.then_inc(s["gateT_done"], 1)
            pe.wait_ge(s["nchunk_ready"], 1)
            mm(ps[0:1, 5, 0:EXPERTS + 1], nchunk[:, 0:1], k("before_e")[0:EXPERTS, :], start=True, stop=True)
            mm(ps[0:1, 5, EXPERTS + 1:2 * EXPERTS + 1], nchunk[:, 0:1], ident[0:EXPERTS, 0:EXPERTS],
               start=True, stop=True)\
                .then_inc(s["base_done"], 1)
            pe.wait_ge(s["gateT_ready"], 1)
            pe.wait_ge(bias_in, 32)
            for t in range(TT):
                for h in range(2):
                    last = mm(ps[:, 2 * t + h, :], gateT[:, t * P:(t + 1) * P], bdn_sb[:, h * BANK:(h + 1) * BANK],
                              start=True, stop=True)
            last.then_inc(s["bias_done"], 1)
            pe.wait_ge(s["rank_ready"], 1)
            spread_over(2, 6)
            pe.wait_ge(s["spread_ready"], 2)
            pe.wait_ge(m["acc_ready"], 1)

            def gather(g):
                pe.wait_ge(m["pick_ready"], g + 1)
                for b in range(DB):
                    for t in range(TT):
                        last = mm(ps[:, GATHER, b * CAP:(b + 1) * CAP], xn2[:, t, b * P:(b + 1) * P],
                                  pick[:, t, :], start=(t == 0), stop=(t == TT - 1))
                last.then_inc(m["gathered"], 1)

            def turn_pick(g):
                for t in range(TT):
                    last = nc.tensor.transpose(ps[:, DOWN, t * P:(t + 1) * P], pickg[:, t, :], ident)
                last.then_inc(m["pick_turned"], 1)

            def scatter(g):
                ge(pe, m["ye_ready"], g)
                ge(pe, m["pickT_ready"], g)
                for t in range(TT):
                    for h in range(2):
                        last = mm(ps[:, TURN + 2 * t + h, :], pickT[CAP * h:CAP * h + CAP, t * P:(t + 1) * P],
                                  ye[CAP * h:CAP * h + CAP, :], start=True, stop=True)
                last.then_inc(m["scattered"], 1)

            def down(g, e):
                pe.wait_ge(m["act_ready"], g)
                for j in range(4):
                    last = nc.tensor.transpose(ps[:, TURN, j * P:(j + 1) * P], act_sb[:, j * P:(j + 1) * P], ident)
                last.then_inc(m["turned"], 1)
                pe.wait_ge(m["actT_ready"], g)
                arrivals = list(expert_units(GU_UNITS, DN_UNITS, e))
                for fb in range(DB):
                    at, count = arrivals[fb // 2]
                    if fb % 2 == 0:
                        pe.wait_ge(unit_in[at], count)
                    w = ring[:, at, :].rearrange("p (k n) -> p k n", n=D)
                    lhs = actT[:, fb % 4, (fb // 4) * CAP:(fb // 4 + 1) * CAP]
                    for h in range(2):
                        last = mm(ps[CAP * h:CAP * h + CAP, DOWN, :], lhs, w[:, fb % 2, h * BANK:(h + 1) * BANK],
                                  start=(fb == 0), stop=(fb == DB - 1))
                last.then_inc(m["down_done"], 1)

            def gate_up(g, e, first=False):
                outs = [(ps[CAP * h:CAP * h + CAP, bank, :], (2 * bank + h) * BANK)
                        for bank in (GATE, UP) for h in range(2)]
                for o, c0 in outs:
                    mm(o, esel[:, :], bgu_sb[:, c0:c0 + BANK], start=True, stop=False)
                pe.wait_ge(m["xg_ready"], g + 1)
                for kk, (at, count) in enumerate(expert_units(0, GU_UNITS, e)):
                    pe.wait_ge(unit_in[at], count)
                    for o, c0 in outs:
                        last = mm(o, xg[:, kk, :], ring[:, at, c0:c0 + BANK], start=False, stop=(kk == DB - 1))
                    if kk == 1:
                        if not first:
                            scatter(g)
                        turn_pick(g)
                last.then_inc(m["gu_done"], 1)

            def chunk(g, e, e_before):
                gather(g)
                down(g, e_before)
                gate_up(g, e)

            pe.wait_ge(s["base_ready"], 1)

            def more_chunks(e):
                b0 = pe.value_load(base[0:1, bass.ds(e, 1)], min_val=0, max_val=MAX_CHUNKS)
                n = pe.value_load(base[0:1, bass.ds(e + EXPERTS + 1, 1)], min_val=1, max_val=CHUNKS)
                with pe.If(n > 1):
                    with pe.Fori(1, n) as c:
                        chunk(b0 + c, e, e)

            gather(0)
            gate_up(0, 0, first=True)
            more_chunks(0)
            with pe.Fori(1, EXPERTS) as e:
                b0 = pe.value_load(base[0:1, bass.ds(e, 1)], min_val=1, max_val=MAX_CHUNKS)
                chunk(b0, e, e - 1)
                more_chunks(e)
            n = pe.value_load(base[0:1, EXPERTS:EXPERTS + 1], min_val=EXPERTS, max_val=MAX_CHUNKS)
            down(n, EXPERTS - 1)
            scatter(n)

        @block.scalar
        def _(act):
            A = nc.scalar.activation
            steps = [0]

            def link(ins):
                steps[0] += 1
                ins.then_inc(s["act_step"], 1)
                act.wait_ge(s["act_step"], steps[0])

            for name, src in (("ada_b", ada_b), ("pre1_g", pre1_g), ("post1_g", post1_g), ("pre2_g", pre2_g),
                              ("post2_g", post2_g), ("c", c)):
                lo, hi = ROWS[name]
                act.dma_start(rows[lo:hi, :], src[0].rearrange("(r p) -> r p", p=P)).then_inc(rows_in, 16)
            for name, src in (("pool_b", pool_b), ("pool_scale", pool_scale)):
                lo, hi = ROWS[name]
                act.dma_start(rows[lo:hi, :], src[0].rearrange("g n -> (g n)").rearrange("(r p) -> r p", p=P))\
                    .then_inc(rows_in, 16)

            def small_loads():
                act.dma_start(poolw_sb[:, :, :], pool_w[0].rearrange("g n d -> (g n) d")
                              .rearrange("(b p) d -> p b d", p=P)).then_inc(poolw_in, 16)
                act.dma_start(rw_sb[:, :, :], router_w[0].rearrange("(k p) e -> p k e", p=P)).then_inc(router_in, 16)
                act.dma_start(rb_sb[:, :], router_b).then_inc(router_in, 16)
                act.dma_start(bgu_sb[:, :], b_gu[0]).then_inc(bias_in, 16)
                act.dma_start(bdn_sb[:, :], b_dn[0]).then_inc(bias_in, 16)

            def square_sums(src, at, done):
                for t in range(TT):
                    link(A(junk, src[:, t, :], ACT.Square, accum_out=stat[:, at + t:at + t + 1]))
                nc.scalar.activation(stat[:, 12:13], stat[:, at:at + 1], ACT.Copy).then_inc(s[done], 1)

            def std(n, at):
                act.wait_ge(s["var_ready"], n)
                A(stat[:, at:at + TT], stat[:, at:at + TT], ACT.Sqrt).then_inc(s["std_ready"], 1)

            def normed(n, at, src, dst, done):
                act.wait_ge(s["rstd_ready"], n)
                for t in range(TT):
                    A(dst[:, t, :], src[:, t, :], ACT.Copy, scale=stat[:, at + t:at + t + 1]).then_inc(s[done], 1)

            act.wait_ge(x_in, 16)
            square_sums(x_sb, 0, "squares_ready")
            std(1, 0)
            normed(1, 0, x_sb, xhat, "xhat_ready")
            act.wait_ge(s["cols_ready"], 1)
            A(csig[:, :], col("c"), ACT.Sigmoid).then_inc(s["csig_ready"], 1)
            small_loads()

            def affine(n, f, shift, done):
                for b in range(4, DB):
                    last = A(hT[:, b, :], xT_ps[:, b, :], ACT.Identity, scale=fac[:, f, b:b + 1],
                             bias=mod[:, shift + b:shift + b + 1])
                last.then_inc(s[done], 1)

            act.wait_ge(s["x_turned"], 1)
            act.wait_ge(s["mod_ready"], 1)
            affine(1, 0, 0, "hT_ready")
            for n, scale in ((0, HD ** -0.5), (1, 1.0)):
                if n == 0:
                    act.wait_ge(s["q_done"], 1)
                else:
                    used(act, "w_in", 1)
                A(qkT[:, 2 * n:2 * n + 2, :], ps[:, 6 + n, :].rearrange("p (b t) -> p b t", t=SEQ), ACT.Copy,
                  scale=scale).then_inc(s["qk_ready"], 1)
            z0, z1 = ps[:, 4:6, :], ps[:, 6:8, 0:SEQ]
            e0v, e1v = e0.rearrange("p (a n) -> p a n", a=2), e1.rearrange("p (a n) -> p a n", a=2)
            act.wait_ge(s["z_done"], 1)
            A(e0v, z0, ACT.Abs).then_inc(s["act_step"], 1)
            A(e1v, z1, ACT.Abs).then_inc(s["act_step"], 1)
            steps[0] += 2
            act.wait_ge(s["act_step"], steps[0])
            for func, scale, bias in ((ACT.Exp, -1.0, 0.0), (ACT.Ln, 1.0, 1.0)):
                link(A(area2[:, 1536:3072], area2[:, 1536:3072], func, scale=scale, bias=bias))
            A(stat[:, 13:14], stat[:, 0:1], ACT.Copy).then_inc(s["sp_part"], 1)

            def gate_block(n):
                for t in range(TT):
                    in_block_done(act, n, t)
                    A(gates[:, t, (n - 3) * BANK:(n - 2) * BANK], ps[:, 2 * ((n - 1) % 2) + t, :], ACT.Sigmoid)\
                        .then_inc(s["gates_ready"], 1)

            gate_block(3)
            gate_block(4)
            act.wait_ge(s["loga_done"], 1)
            A(a0, z0.rearrange("p a (b q) -> p a b q", b=2), ACT.Exp).then_inc(s["a_ready"], 1)
            A(a1, z1.rearrange("p a (b q) -> p a b q", b=2), ACT.Exp).then_inc(s["a_ready"], 1)
            gate_block(5)
            act.wait_ge(s["o_done"], 1)
            A(attnT[:, :, :], ps[:, 4, :].rearrange("p (b t) -> p b t", t=SEQ), ACT.Copy)\
                .then_inc(s["attnT_ready"], 1)
            gate_block(6)
            act.wait_ge(s["m_turned"], 1)
            for n in range(2):
                last = A(hT[:, 4 + 2 * n:6 + 2 * n, :], ps[:, 6 + n, :].rearrange("p (b t) -> p b t", t=SEQ), ACT.Copy)
            last.then_inc(s["mT_ready"], 1)
            y_ps = ps[:, 0:4, :].rearrange("p (t h) n -> p t (h n)", t=TT)
            used(act, "w_out", 3)
            for t in range(TT):
                link(A(tail[:, t, :], y_ps[:, t, :], ACT.Square, accum_out=stat[:, 2 + t:3 + t]))
            A(stat[:, 12:13], stat[:, 2:3], ACT.Copy).then_inc(s["squares_ready"], 1)
            std(2, 2)
            act.wait_ge(s["x1_ready"], 1)
            for t in range(TT):
                link(A(tail[:, t, :], x_sb[:, t, :], ACT.Square, accum_out=stat[:, 4 + t:5 + t]))
            A(stat[:, 12:13], stat[:, 4:5], ACT.Copy).then_inc(s["squares_ready"], 1)
            std(3, 4)
            normed(3, 4, x_sb, xn2, "xn2_ready")
            act.wait_ge(s["x2_turned"], 1)
            act.wait_ge(s["mod_ready"], 3)
            affine(2, 2, 3 * DB, "h2_ready")
            act.wait_ge(s["logit_ready"], 1)
            for t in range(TT):
                last = A(top_e[:, t, :], top_f[:, t, :], ACT.Exp)
            last.then_inc(s["exp_ready"], 1)
            act.wait_ge(s["gateT_done"], 1)
            A(gateT[:, :], ps[0:EXPERTS, 6, 0:SEQ], ACT.Copy).then_inc(s["gateT_ready"], 1)
            act.wait_ge(s["bias_done"], 1)
            A(yacc[:, :, :], y_ps, ACT.Copy).then_inc(m["acc_ready"], 1)

            def back(g):
                act.wait_ge(m["gmin_ready"], g)
                A(g_sig, g_min, ACT.Sigmoid, scale=ALPHA).then_inc(m["sig_ready"], 1)
                act.wait_ge(m["turned"], g)
                A(actT, ps[:, TURN, :].rearrange("p (j s) -> p j s", s=P), ACT.Copy).then_inc(m["actT_ready"], 1)
                act.wait_ge(m["down_done"], g)
                A(ye, ps[:, DOWN, :], ACT.Copy).then_inc(m["ye_ready"], 1)

            def front(g):
                act.wait_ge(m["pick_turned"], g + 1)
                A(pickT, ps[:, DOWN, 0:2 * P], ACT.Copy).then_inc(m["pickT_ready"], 1)

            act.wait_ge(s["base_ready"], 1)

            def more_chunks(e):
                b0 = act.value_load(base[0:1, bass.ds(e, 1)], min_val=0, max_val=MAX_CHUNKS)
                n = act.value_load(base[0:1, bass.ds(e + EXPERTS + 1, 1)], min_val=1, max_val=CHUNKS)
                with act.If(n > 1):
                    with act.Fori(1, n) as c:
                        back(b0 + c)
                        front(b0 + c)

            front(0)
            more_chunks(0)
            with act.Fori(1, EXPERTS) as e:
                b0 = act.value_load(base[0:1, bass.ds(e, 1)], min_val=1, max_val=MAX_CHUNKS)
                back(b0)
                front(b0)
                more_chunks(e)
            n = act.value_load(base[0:1, EXPERTS:EXPERTS + 1], min_val=EXPERTS, max_val=MAX_CHUNKS)
            back(n)
            act.wait_ge(m["acc_ready"], n + 1)
            for t in range(TT):
                link(A(tail[:, t, :], yacc[:, t, :], ACT.Square, accum_out=stat[:, 6 + t:7 + t]))
            A(stat[:, 12:13], stat[:, 6:7], ACT.Copy).then_inc(s["squares_ready"], 1)
            std(4, 6)

        @block.gpsimd
        def _(pool):
            def causal(tile, width, done):
                nc.gpsimd.affine_select(out=tile, in_=tile, compare_op=ALU.is_gt, fill=0.0, base=0,
                                        pattern=[[0, 2], [0, 2], [1, width]], channel_multiplier=-1).then_inc(done, 1)

            pool.wait_ge(s["sp_ready"], 2)
            causal(sp0, SEQ, s["sp_masked"])
            causal(sp1, P, s["sp_masked"])
            pool.wait_ge(s["a_ready"], 2)
            causal(a0, SEQ, s["a_masked"])
            causal(a1, P, s["a_masked"])

        @block.vector
        def _(dve):
            V = nc.vector
            steps = [0]

            def link(ins):
                steps[0] += 1
                ins.then_inc(s["dve_step"], 1)
                dve.wait_ge(s["dve_step"], steps[0])

            def variance(n, at):
                dve.wait_ge(s["squares_ready"], n)
                V.tensor_scalar(stat[:, at:at + TT], stat[:, at:at + TT], 1.0 / D, EPS, ALU.mult, ALU.add)\
                    .then_inc(s["var_ready"], 1)

            def rstd(n, at, done=True):
                dve.wait_ge(s["std_ready"], n)
                ins = V.reciprocal(stat[:, at:at + TT], stat[:, at:at + TT])
                if done:
                    ins.then_inc(s["rstd_ready"], 1)
                else:
                    link(ins)

            def over(ap, n):
                return ap.unsqueeze(2).broadcast_to([ap.shape[0], ap.shape[1], n])

            dve.wait_ge(s["rows_turned"], 1)
            V.tensor_copy(cols[:, :], ps[:, 5, 0:N_ROWS]).then_inc(s["cols_ready"], 1)
            variance(1, 0)
            rstd(1, 0)
            dve.wait_ge(s["csig_ready"], 1)
            dve.wait_ge(s["cols_ready"], 1)
            V.tensor_tensor(cact[:, :, :], over(col("c"), 32), over(csig[:, :], 32), ALU.mult)\
                .then_inc(s["cact_ready"], 1)

            def mod_rows(j, bank):
                used(dve, f"ada{j}", DB - 1)
                V.tensor_copy(modrow[:, :], ps[:, bank, :]).then_inc(s["modrow_ready"], 1)

            def mod_cols(j, bank):
                dve.wait_ge(s["modcol_done"], j + 1)
                link(V.tensor_tensor(mod[:, 16 * j:16 * j + 16], ps[:, bank, 0:16], col("ada_b", 16 * j, 16 * j + 16),
                                     ALU.add))

            def factor(f, at, gain, plus):
                return V.scalar_tensor_tensor(out=fac[:, f, :], in0=mod[:, at:at + DB], scalar=plus, in1=col(gain),
                                              op0=ALU.add, op1=ALU.mult)

            def affine(f, shift, done):
                for b in range(4):
                    last = V.tensor_scalar(hT[:, b, :], xT_ps[:, b, :], fac[:, f, b:b + 1],
                                           mod[:, shift + b:shift + b + 1], ALU.mult, ALU.add)
                last.then_inc(s[done], 1)

            mod_rows(0, 4)
            mod_cols(0, 5)
            link(factor(0, DB, "pre1_g", 1.0))
            V.tensor_copy(stat[:, 14:15], stat[:, 0:1]).then_inc(s["mod_ready"], 1)
            dve.wait_ge(s["x_turned"], 1)
            affine(0, 0, "hT_ready")
            for n in (1, 2):
                for t in range(TT):
                    in_block_done(dve, n, t)
                    V.tensor_copy(vu[:, t, (n - 1) * BANK:n * BANK], ps[:, 2 * (n - 1) + t, :])\
                        .then_inc(s["vu_ready"], 1)
            z0, z1 = ps[:, 4:6, :], ps[:, 6:8, 0:SEQ]
            dve.wait_ge(s["sp_part"], 1)
            V.scalar_tensor_tensor(out=area2[:, 0:1024].rearrange("p (a n) -> p a n", a=2), in0=z0, scalar=0.0,
                                   in1=e0.rearrange("p (a n) -> p a n", a=2), op0=ALU.max, op1=ALU.add)\
                .then_inc(s["sp_ready"], 1)
            V.scalar_tensor_tensor(out=area2[:, 1024:1536].rearrange("p (a n) -> p a n", a=2), in0=z1, scalar=0.0,
                                   in1=e1.rearrange("p (a n) -> p a n", a=2), op0=ALU.max, op1=ALU.add)\
                .then_inc(s["sp_ready"], 1)
            dve.wait_ge(s["mix_done"], 1)
            V.tensor_copy(mixT, ps[:, 5:8, :].rearrange("p k (b t) -> p (k b) t", t=SEQ)).then_inc(s["mixT_ready"], 1)
            dve.wait_ge(s["pool_done"], 1)
            for b in range(PB):
                last = V.tensor_scalar(poolT[:, b, :], ps[:, 5 + b // 2, (b % 2) * SEQ:(b % 2 + 1) * SEQ],
                                       col("pool_b", b, b + 1), col("pool_scale", b, b + 1), ALU.add, ALU.mult)
            last.then_inc(s["poolT_ready"], 1)
            for t in range(TT):
                for h in range(2):
                    branch_done(dve, s["brA_done"], "br_attn", 0, t, h)
                    V.tensor_tensor(merged[:, t, h * BANK:(h + 1) * BANK], ps[:, 2 * t + h, :],
                                    gates[:, t, h * BANK:(h + 1) * BANK], ALU.mult).then_inc(s["brA_ready"], 1)
            for t in range(TT):
                for h in range(2):
                    branch_done(dve, s["brP_done"], "br_pool", 2, t, h)
                    link(V.tensor_tensor(prod[:, h, :], ps[:, 4 + 2 * t + h, :],
                                         gates[:, t, D + h * BANK:D + (h + 1) * BANK], ALU.mult))
                    half = merged[:, t, h * BANK:(h + 1) * BANK]
                    V.tensor_tensor(half, half, prod[:, h, :], ALU.add).then_inc(s["brP_ready"], 1)
            mod_rows(1, 0)
            dve.wait_ge(s["m_turned"], 1)
            V.tensor_copy(hT[:, 0:4, :], ps[:, 4:6, :].rearrange("p k (b t) -> p (k b) t", t=SEQ))\
                .then_inc(s["mT_ready"], 1)
            mod_cols(1, 4)
            link(factor(1, 2 * DB, "post1_g", 0.0))
            V.tensor_copy(stat[:, 14:15], stat[:, 0:1]).then_inc(s["mod_ready"], 1)

            def diagonal(f):
                V.tensor_tensor(diag, ident.unsqueeze(1).broadcast_to([P, DB, P]), over(fac[:, f, :], P), ALU.mult)\
                    .then_inc(s["diag_ready"], 1)

            def spread_read(n, bank):
                dve.wait_ge(s["spread_done"], n)
                ins = V.tensor_copy(spread[:, :].rearrange("p (h n) -> p h n", h=2), ps[:, bank:bank + 2, :])
                ins.then_inc(s["spread_ready"], 1)

            diagonal(1)
            spread_read(1, 6)
            mod_rows(2, 5)
            y_ps = ps[:, 0:4, :].rearrange("p (t h) n -> p t (h n)", t=TT)
            variance(2, 2)
            rstd(2, 2, done=False)
            dve.wait_ge(s["spread_ready"], 1)
            for t in range(TT):
                link(V.scalar_tensor_tensor(out=tail[:, t, :], in0=y_ps[:, t, :], scalar=stat[:, 2 + t:3 + t],
                                            in1=spread[:, :], op0=ALU.mult, op1=ALU.mult))
            for t in range(TT):
                link(V.tensor_tensor(x_sb[:, t, :], x_sb[:, t, :], tail[:, t, :], ALU.add))
            V.tensor_copy(stat[:, 14:15], stat[:, 0:1]).then_inc(s["x1_ready"], 1)
            mod_cols(2, 4)
            link(factor(2, 4 * DB, "pre2_g", 1.0))
            link(factor(3, 5 * DB, "post2_g", 0.0))
            V.tensor_copy(stat[:, 14:15], stat[:, 0:1]).then_inc(s["mod_ready"], 1)
            diagonal(3)
            variance(3, 4)
            dve.wait_ge(s["std_ready"], 3)
            V.reciprocal(stat[:, 4:4 + TT], stat[:, 4:4 + TT]).then_inc(s["rstd_ready"], 2)
            dve.wait_ge(s["x2_turned"], 1)
            affine(2, 3 * DB, "h2_ready")
            dve.wait_ge(s["logit_done"], 1)
            link(V.tensor_copy(logit[:, :, :], ps[:, 5, 0:TT * EXPERTS].rearrange("p (t e) -> p t e", t=TT)))
            for t in range(TT):
                link(V.max(top_v[:, t, :], logit[:, t, :]))
                link(V.max_index(top_i[:, t, :], top_v[:, t, :], logit[:, t, :]))
                link(V.tensor_scalar(top_f[:, t, :], top_v[:, t, 0:TOP_K], top_v[:, t, 0:1], None, ALU.subtract))
            V.tensor_copy(stat[:, 14:15], stat[:, 0:1]).then_inc(s["logit_ready"], 1)
            link(V.tensor_copy(top_g[:, :, :], top_i[:, :, 0:TOP_K]))
            for t in range(TT):
                link(V.tensor_tensor(hot[:, t], k("expert").unsqueeze(1).broadcast_to([P, TOP_K, EXPERTS]),
                                     over(top_g[:, t, :], EXPERTS), ALU.is_equal))
                link(V.tensor_reduce(mask[:, t, :], hot[:, t].rearrange("p r e -> p e r"), AX.X, ALU.add))
            V.tensor_copy(stat[:, 14:15], stat[:, 0:1]).then_inc(s["mask_ready"], 1)
            dve.wait_ge(s["exp_ready"], 1)
            for t in range(TT):
                link(V.tensor_reduce(stat[:, 8 + t:9 + t], top_e[:, t, :], AX.X, ALU.add))
            link(V.reciprocal(stat[:, 8:8 + TT], stat[:, 8:8 + TT]))
            for t in range(TT):
                link(V.tensor_scalar(top_e[:, t, :], top_e[:, t, :], stat[:, 8 + t:9 + t], None, ALU.mult))
                link(V.tensor_tensor(hotg[:, t], hot[:, t], over(top_e[:, t, :], EXPERTS), ALU.mult))
                link(V.tensor_reduce(gate[:, t, :], hotg[:, t].rearrange("p r e -> p e r"), AX.X, ALU.add))
            V.tensor_copy(stat[:, 14:15], stat[:, 0:1]).then_inc(s["gate_ready"], 1)
            dve.wait_ge(s["count_done"], 1)
            count = ps[0:EXPERTS, 4, 0:1]
            link(V.tensor_scalar(nchunk[:, 1:2], count, float(CAP), 1.0, ALU.is_gt, ALU.add))
            for n in range(2, CHUNKS):
                link(V.scalar_tensor_tensor(out=nchunk[:, n % 2:n % 2 + 1], in0=count, scalar=float(n * CAP),
                                            in1=nchunk[:, 1 - n % 2:2 - n % 2], op0=ALU.is_gt, op1=ALU.add))
            link(V.tensor_copy(nchunk[:, 0:1], nchunk[:, (CHUNKS - 1) % 2:(CHUNKS - 1) % 2 + 1]))
            V.tensor_copy(stat[:, 14:15], stat[:, 0:1]).then_inc(s["nchunk_ready"], 1)
            dve.wait_ge(s["rank_done"], 1)
            link(V.scalar_tensor_tensor(out=rank[:, :, :], in0=ps[:, 7, 0:TT * EXPERTS]
                                        .rearrange("p (t e) -> p t e", t=TT), scalar=1.0, in1=mask[:, :, :],
                                        op0=ALU.add, op1=ALU.mult))
            V.tensor_scalar(rank[:, :, :], rank[:, :, :], -1.0, None, ALU.add).then_inc(s["rank_ready"], 1)
            dve.wait_ge(s["base_done"], 1)
            V.tensor_copy(base[:, :], ps[0:1, 5, 0:2 * EXPERTS + 1]).then_inc(s["base_ready"], 1)
            spread_read(2, 6)
            dve.wait_ge(s["rank_ready"], 1)
            dve.wait_ge(s["base_ready"], 1)

            def picks(g, e, c):
                ge(dve, m["pick_turned"], g)
                for t in range(TT):
                    r = rank[:, t, bass.ds(e, 1)]
                    V.tensor_scalar(pick[:, t, :], slot[:, bass.ds(c, 1), 0:CAP].rearrange("p o s -> p (o s)"),
                                    r, None, ALU.is_equal)
                    if t == 0:
                        V.tensor_copy(esel[:, :], ident[0:EXPERTS, bass.ds(e, 1)].broadcast_to([EXPERTS, CAP]))
                    last = V.tensor_scalar(pickg[:, t, :], slot[:, bass.ds(c, 1), :].rearrange("p o s -> p (o s)"),
                                           r, gate[:, t, bass.ds(e, 1)], ALU.is_equal, ALU.mult)
                last.then_inc(m["pick_ready"], 1)

            def activate(g):
                dve.wait_ge(m["gu_done"], g)
                V.tensor_scalar(g_min, ps[:, GATE, :], LIMIT, None, ALU.min).then_inc(m["gmin_ready"], 1)
                V.tensor_scalar(u_clip, ps[:, UP, :], LIMIT, -LIMIT, ALU.min, ALU.max).then_inc(m["u_ready"], 1)
                dve.wait_ge(m["sig_ready"], g)
                V.tensor_tensor(g_act, g_min, g_sig, ALU.mult).then_inc(m["gact_ready"], 1)
                dve.wait_ge(m["gact_ready"], g)
                dve.wait_ge(m["u_ready"], g)
                V.scalar_tensor_tensor(out=act_sb, in0=u_clip, scalar=1.0, in1=g_act, op0=ALU.add, op1=ALU.mult)\
                    .then_inc(m["act_ready"], 1)

            def affine_gathered(g):
                dve.wait_ge(m["gathered"], g + 1)
                V.tensor_tensor(xg_m, ps[:, GATHER, :].rearrange("p (b s) -> p b s", s=CAP),
                                over(fac[:, 2, :], CAP), ALU.mult).then_inc(m["xgm_ready"], 1)
                dve.wait_ge(m["xgm_ready"], g + 1)
                V.tensor_tensor(xg, xg_m, over(mod[:, 3 * DB:4 * DB], CAP), ALU.add).then_inc(m["xg_ready"], 1)

            def accumulate(g):
                dve.wait_ge(m["scattered"], g)
                dve.wait_ge(m["acc_ready"], g)
                last = V.tensor_tensor(yacc[:, :, :], yacc[:, :, :],
                                       ps[:, TURN:8, :].rearrange("p (t h) n -> p t (h n)", t=TT), ALU.add)
                last.then_inc(m["acc_ready"], 1)

            def more_chunks(e):
                b0 = dve.value_load(base[0:1, bass.ds(e, 1)], min_val=0, max_val=MAX_CHUNKS)
                n = dve.value_load(base[0:1, bass.ds(e + EXPERTS + 1, 1)], min_val=1, max_val=CHUNKS)
                with dve.If(n > 1):
                    with dve.Fori(1, n) as c:
                        picks(b0 + c, e, c)
                        activate(b0 + c)
                        affine_gathered(b0 + c)
                        accumulate(b0 + c)

            picks(0, 0, 0)
            affine_gathered(0)
            more_chunks(0)
            with dve.Fori(1, EXPERTS) as e:
                b0 = dve.value_load(base[0:1, bass.ds(e, 1)], min_val=1, max_val=MAX_CHUNKS)
                picks(b0, e, 0)
                activate(b0)
                affine_gathered(b0)
                accumulate(b0)
                more_chunks(e)
            n = dve.value_load(base[0:1, EXPERTS:EXPERTS + 1], min_val=EXPERTS, max_val=MAX_CHUNKS)
            activate(n)
            accumulate(n)
            variance(4, 6)
            rstd(4, 6, done=False)
            dve.wait_ge(s["spread_ready"], 2)
            for t in range(TT):
                link(V.scalar_tensor_tensor(out=tail[:, t, :], in0=yacc[:, t, :], scalar=stat[:, 6 + t:7 + t],
                                            in1=spread[:, :], op0=ALU.mult, op1=ALU.mult))
                V.tensor_tensor(tail[:, t, :], tail[:, t, :], x_sb[:, t, :], ALU.add).then_inc(s["out_done"], 1)


_INS = ["x", "c", "ada_w", "ada_b", "pre1_g", "post1_g", "pre2_g", "post2_g", "w_in", "pool_w", "pool_b",
        "pool_scale", "w_br_attn", "w_br_pool", "w_out", "router_w", "router_b", "w_gu", "b_gu", "w_dn", "b_dn"]


def constants(np):
    v = np.zeros((P, CONST_W), np.float32)
    row, colm = np.arange(P)[:, None], np.arange(P)[None, :]

    def put(name, value):
        a, b = CONSTS[name]
        v[:, a:b] = value

    put("ident", row == colm)
    put("tri_neg", np.where(row >= colm, -1.0, 0.0))
    put("ones_neg", -1.0)
    put("before", row < colm)
    put("ones", 1.0)
    tok, query = np.arange(SEQ)[:, None], np.arange(SEQ)[None, :]
    bands = []
    for w in WINDOWS:
        inside = (query - tok >= 0) & (query - tok < w)
        bands.append(np.where(inside, 1.0 / np.minimum(query + 1, w), 0.0) - (query == tok))
    put("band0", np.concatenate([b[0:P] for b in bands], axis=1))
    put("band1", np.concatenate([b[P:SEQ, P:SEQ] for b in bands], axis=1))
    put("slot", np.concatenate([CAP * n + np.arange(P) % CAP for n in range(CHUNKS)])[None, :])
    put("expert", np.arange(EXPERTS)[None, :])
    put("before_e", row < np.arange(EXPERTS + 1)[None, :])
    put("quad", row == 32 * np.arange(4)[None, :])
    return v


def kernel(**inputs):
    import numpy as np
    import concourse.bacc as bacc
    from concourse.bass_utils import run_bass_kernel_spmd

    nc = bacc.Bacc("TRN2", target_bir_lowering=False, num_devices=1)
    arrays, args = {}, []
    for name in _INS:
        a = np.ascontiguousarray(inputs[name])
        arrays[f"in_{name}"] = a
        args.append(nc.dram_tensor(f"in_{name}", a.shape, mybir.dt.from_np(a.dtype), kind="ExternalInput").ap())
    table = constants(np)
    arrays["in_consts"] = table
    args.append(nc.dram_tensor("in_consts", table.shape, mybir.dt.float32, kind="ExternalInput").ap())
    args.append(nc.dram_tensor("out_0", (1, SEQ, D), mybir.dt.float32, kind="ExternalOutput").ap())
    build(nc, *args)
    r = run_bass_kernel_spmd(nc, [arrays], core_ids=[0])
    return r.results[0]["out_0"]
```

```python
import concourse.bass as bass
from concourse import mybir
from contextlib import ExitStack

P = 128
SEQ, D = 256, 1024
TT = SEQ // P
DB = D // P
BANK = 512
HEADS, HD = 4, 64
ATTN_W = HEADS * HD
POOL_W = D - ATTN_W
WINDOWS = (2, 4, 8, 16)
GROUP = POOL_W // len(WINDOWS)
PB = POOL_W // P
IN_W = 3 * ATTN_W + POOL_W + 2 * D
EXPERTS, TOP_K = 32, 4
F = D
CAP = 64
CHUNKS = SEQ // CAP
MAX_CHUNKS = EXPERTS + SEQ * TOP_K // CAP
LIMIT, ALPHA, EPS = 7.0, 1.702, 1e-6

CONSTS = {}
_at = 0
for _name, _width in (("ident", P), ("ones", P), ("quad", 4), ("tri_neg", P), ("ones_neg", P), ("before", P),
                      ("band0", len(WINDOWS) * SEQ), ("band1", len(WINDOWS) * P),
                      ("slot", CHUNKS * P), ("expert", EXPERTS), ("before_e", EXPERTS + 1), ("passed", CHUNKS - 1)):
    CONSTS[_name] = (_at, _at + _width)
    _at += _width
CONST_W = _at
CONST_FIRST = CONSTS["quad"][1]

ROWS = {}
_at = 0
for _name, _count in (("ada_b", 6 * DB), ("pre1_g", DB), ("post1_g", DB), ("pre2_g", DB),
                      ("post2_g", DB), ("c", DB), ("pool_b", PB), ("pool_scale", PB)):
    ROWS[_name] = (_at, _at + _count)
    _at += _count
N_ROWS = _at

SLOTS, SLOT_W = 12, 2048
MIX_UNITS = ([("ada0", k) for k in range(DB)] + [("w_in", i) for i in range(2 * IN_W // BANK)]
             + [("br_attn", 0)] + [("br_pool", i) for i in range(3)]
             + [("ada1", k) for k in range(DB)] + [("ada2", k) for k in range(DB // 2)]
             + [("w_out", i) for i in range(4)] + [("ada2", k) for k in range(DB // 2, DB)])
N_MIX = len(MIX_UNITS)
GU_UNITS, DN_UNITS = DB, 4
assert GU_UNITS + DN_UNITS == SLOTS


def unit_of(name, i):
    return MIX_UNITS.index((name, i))


def build(nc, x, c, ada_w, ada_b, pre1_g, post1_g, pre2_g, post2_g, w_in, pool_w, pool_b, pool_scale,
          w_br_attn, w_br_pool, w_out, router_w, router_b, w_gu, b_gu, w_dn, b_dn, consts, out):
    f32, i32, u32 = mybir.dt.float32, mybir.dt.int32, mybir.dt.uint32
    ALU = mybir.AluOpType
    ACT = mybir.ActivationFunctionType
    AX = mybir.AxisListType

    ctx = ExitStack()
    with ctx:
        def sb(name, shape, dt=f32):
            return ctx.enter_context(nc.sbuf_tensor(name, shape, dt))

        def sem(name):
            return ctx.enter_context(nc.semaphore(name))

        ring = sb("ring", [P, SLOTS, SLOT_W])
        const = sb("const", [P, CONST_W])
        rows = sb("rows", [N_ROWS, P])
        cols = sb("cols", [P, N_ROWS])
        x_sb = sb("x_sb", [P, TT, D])
        hT = sb("hT", [P, DB, SEQ])
        vu = sb("vu", [P, TT, D])
        merged = sb("merged", [P, TT, D])
        area = sb("area", [P, 4096])
        area2 = sb("area2", [P, 3 * 1536])
        qkT = sb("qkT", [P, 4, SEQ])
        attnT = sb("attnT", [P, 2, SEQ])
        poolw_sb = sb("poolw_sb", [P, PB, GROUP])
        spread = sb("spread", [P, D])
        bgu_sb = sb("bgu_sb", [EXPERTS, 2 * F])
        bdn_sb = sb("bdn_sb", [EXPERTS, D])
        rw_sb = sb("rw_sb", [P, DB, EXPERTS])
        rb_sb = sb("rb_sb", [1, EXPERTS])
        modrow = sb("modrow", [P, BANK])
        mod = sb("mod", [P, 6 * DB])
        fac = sb("fac", [P, 4, DB])
        csig = sb("csig", [P, DB])
        cact = sb("cact", [P, DB, 32])
        stat = sb("stat", [P, 16])
        unread = sb("unread", [P, 8])
        top_v = sb("top_v", [P, TT, 8])
        top_i = sb("top_i", [P, TT, 8], u32)
        top_f = sb("top_f", [P, TT, TOP_K])
        top_e = sb("top_e", [P, TT, TOP_K])
        top_g = sb("top_g", [P, TT, TOP_K])
        logit = sb("logit", [P, TT, EXPERTS])
        logit0 = sb("logit0", [P, EXPERTS])
        mask = sb("mask", [P, TT, EXPERTS])
        gate = sb("gate", [P, TT, EXPERTS])
        rank = sb("rank", [P, TT, EXPERTS])
        gateT = sb("gateT", [EXPERTS, SEQ])
        nchunk = sb("nchunk", [EXPERTS, 4])
        base = sb("base", [1, 3 * EXPERTS + 1], i32)
        esel = sb("esel", [EXPERTS, CAP])

        def k(name):
            a, b = CONSTS[name]
            return const[:, a:b]

        def col(name, a=0, b=None):
            lo, hi = ROWS[name]
            return cols[:, lo + a:(lo + b if b is not None else hi)]

        ident, ones = k("ident"), k("ones")
        band0 = k("band0").rearrange("p (g t) -> p g t", t=SEQ)
        band1 = k("band1").rearrange("p (g t) -> p g t", t=P)
        slot = k("slot").rearrange("p (c s) -> p c s", s=P)
        gates = area[:, :].rearrange("p (t n) -> p t n", t=TT)
        xhat = merged
        sp0 = area2[:, 0:1024].rearrange("p (a b q) -> p a b q", a=2, b=2)
        sp1 = area2[:, 1024:1536].rearrange("p (a b q) -> p a b q", a=2, b=2)
        e0, e1 = area2[:, 1536:2560], area2[:, 2560:3072]
        a0 = area2[:, 3072:4096].rearrange("p (a b q) -> p a b q", a=2, b=2)
        a1 = area2[:, 4096:4608].rearrange("p (a b q) -> p a b q", a=2, b=2)
        mixT = area2[:, 0:1536].rearrange("p (b t) -> p b t", t=SEQ)
        poolT = area2[:, 1536:3072].rearrange("p (b t) -> p b t", t=SEQ)
        prod = area2[:, 3072:3072 + 1024].rearrange("p (a n) -> p a n", a=2)
        diag = area2[:, 0:1024].rearrange("p (b n) -> p b n", n=P)
        junk = area2[:, 3072:4096]
        tail = area2[:, 1024:3072].rearrange("p (t n) -> p t n", t=TT)
        yspread, yacc = vu, merged
        hot = area[:, 0:256].rearrange("p (t r e) -> p t r e", t=TT, r=TOP_K)
        hotg = area[:, 256:512].rearrange("p (t r e) -> p t r e", t=TT, r=TOP_K)
        pick = area[:, 0:128].rearrange("p (t s) -> p t s", t=TT)
        pickg = area[:, 128:384].rearrange("p (t s) -> p t s", t=TT)
        xg = area[:, 384:896].rearrange("p (b s) -> p b s", s=CAP)
        xg_m = area[:, 896:1408].rearrange("p (b s) -> p b s", s=CAP)
        g_min, g_sig = area[:, 1408:1920], area[:, 1920:2432]
        u_clip, g_act, act_sb = area[:, 2432:2944], area[:, 2944:3456], area[:, 3456:3968]
        actT = area2[:, 3072:3584].rearrange("p (j s) -> p j s", s=P)
        ye = area2[:, 3584:4096]
        pickT = area2[:, 4096:4352]

        ps = ctx.enter_context(nc.psum_tensor("ps", [P, 8, BANK], f32))
        xT_ps = ps[:, 0:4, :].rearrange("p k (b t) -> p (k b) t", t=SEQ)
        GATE, UP, GATHER, DOWN, TURN = range(5)

        const_in, rows_in, x_in, poolw_in, router_in, bias_in = map(
            sem, ("const_in", "rows_in", "x_in", "poolw_in", "router_in", "bias_in"))
        unit_in = [sem(f"unit_in{i}") for i in range(SLOTS)]
        unit_used = sem("unit_used")
        names = ("rows_turned", "cols_ready", "csig_ready", "cact_ready", "squares_ready", "var_ready",
                 "std_ready", "rstd_ready", "xhat_ready", "x_turned", "modrow_ready",
                 "modcol_done", "mod_ready", "hT_ready", "q_done", "qk_ready", "in_done", "vu_ready",
                 "gates_ready", "z_done", "sp_part", "sp_ready", "sp_masked", "loga_done", "a_ready",
                 "a_masked", "o_done", "attnT_ready", "mix_done", "mixT_ready", "pool_done", "even_done",
                 "poolT_ready", "brA_done", "brA_ready", "brP_done", "brP_ready", "m_turned",
                 "mT_ready", "diag_ready", "spread_done", "spread_ready", "x1_ready",
                 "xn2_ready", "x2_turned", "h2_ready", "logit_done", "logit_ready", "exp_ready",
                 "mask_ready", "gate_ready", "rank_done", "count_done", "nchunk_ready", "base_done",
                 "base_ready", "gateT_done", "gateT_ready", "bias_done", "dve_step",
                 "act_step", "out_done", "rank_ready", "y0_squared", "y1_spread", "shift_ready", "logit0_done",
                 "logit0_ready", "logits_here", "max_here", "ysum_ready")
        s = {n: sem(n) for n in names}
        names = ("pick_ready", "gathered", "xgm_ready", "xg_ready", "gu_done", "gmin_ready", "sig_ready",
                 "u_ready", "gact_ready", "act_ready", "turned", "actT_ready", "down_done", "ye_ready",
                 "pick_turned", "pickT_ready", "scattered", "acc_ready")
        m = {n: sem(n) for n in names}
        block = ctx.enter_context(nc.Block())

        def slot_of(u):
            return ring[:, u % SLOTS, :]

        def ge(engine, semaphore, value):
            if isinstance(value, int) and value <= 0:
                return
            engine.wait_ge(semaphore, value)

        def expert_units(first, count, e):
            for j in range(first, first + count):
                u = N_MIX + j
                yield u % SLOTS, 16 * (u // SLOTS + 1) + 16 * e

        def used(engine, name, i):
            engine.wait_ge(unit_used, unit_of(name, i) + 1)

        def in_block_done(engine, n, t):
            if t == 0:
                engine.wait_ge(s["in_done"], n)
            else:
                used(engine, "w_in", 2 * n + 1)

        def branch_done(engine, semaphore, name, i, t, h):
            if (t, h) != (1, 1):
                engine.wait_ge(semaphore, 2 * t + h + 1)
            else:
                used(engine, name, i)

        @block.sync
        def _(sp):
            sp.dma_start(const[:, 0:CONST_FIRST], consts[:, 0:CONST_FIRST]).then_inc(const_in, 16)
            sp.dma_start(x_sb[:, :, :], x[0].rearrange("(t p) n -> p t n", p=P)).then_inc(x_in, 16)
            sp.wait_ge(rows_in, 16 * len(ROWS))
            ada_v = ada_w[0].rearrange("(k p) n -> p k n", p=P)
            win_v = w_in[0].rearrange("(k p) n -> p k n", p=P)
            for u, (name, i) in enumerate(MIX_UNITS):
                dst = slot_of(u)
                if name.startswith("ada"):
                    j = int(name[3])
                    src = ada_v[:, i, j * 2 * D:(j + 1) * 2 * D]
                elif name == "w_in":
                    n, half = i // 2, i % 2
                    dst = dst.rearrange("p (k n) -> p k n", n=BANK)
                    src = win_v[:, 4 * half:4 * half + 4, n * BANK:(n + 1) * BANK]
                else:
                    w = {"br_attn": w_br_attn, "br_pool": w_br_pool, "w_out": w_out}[name]
                    dst = dst.rearrange("p (k n) -> p k n", n=D)
                    src = w[0].rearrange("(k p) n -> p k n", p=P)[:, 2 * i:2 * i + 2, :]
                ge(sp, unit_used, u - SLOTS + 1)
                sp.dma_start(dst, src).then_inc(unit_in[u % SLOTS], 16)

            def expert(e):
                for j in range(SLOTS):
                    u = N_MIX + j
                    if j < GU_UNITS:
                        dst, src = slot_of(u), w_gu[0, e, j * P:(j + 1) * P, :]
                    else:
                        i = j - GU_UNITS
                        dst = slot_of(u).rearrange("p (k n) -> p k n", n=D)
                        src = w_dn[0, e, 2 * i * P:2 * (i + 1) * P, :].rearrange("(k p) n -> p k n", p=P)
                    sp.wait_ge(unit_used, u - SLOTS + 1 + SLOTS * e)
                    sp.dma_start(dst, src).then_inc(unit_in[u % SLOTS], 16)

            expert(0)
            with sp.Fori(1, EXPERTS) as e:
                expert(e)
            for t in range(TT):
                sp.wait_ge(s["out_done"], t + 1)
                sp.dma_start(out[0, t * P:(t + 1) * P, :], tail[:, t, :]).then_inc(x_in, 16)
            sp.wait_ge(x_in, 16 * (1 + TT))

        @block.tensor
        def _(pe):
            mm = nc.tensor.matmul

            def arrived(u):
                pe.wait_ge(unit_in[u % SLOTS], 16 * (u // SLOTS + 1))

            def ada_rows(j, bank, k0, k1):
                for kk in range(k0, k1):
                    u = unit_of(f"ada{j}", kk)
                    arrived(u)
                    for q in range(4):
                        last = mm(ps[32 * q:32 * q + 32, bank, :], cact[:, kk, :],
                                  slot_of(u)[:, q * BANK:(q + 1) * BANK], start=(kk == 0), stop=(kk == DB - 1))
                    last.then_inc(unit_used, 1)

            def ada_cols(j, bank):
                pe.wait_ge(s["modrow_ready"], j + 1)
                view = ps[:, bank, 0:16].rearrange("p (q i) -> p i q", i=4)
                for i in range(4):
                    last = mm(view[:, i, :], modrow[:, i * P:(i + 1) * P], k("quad"), start=True, stop=True)
                last.then_inc(s["modcol_done"], 1)

            def spread_over(n, bank):
                pe.wait_ge(s["diag_ready"], n)
                for h in range(2):
                    last = mm(ps[:, bank + h, :], ones, diag[:, 4 * h:4 * h + 4, :], start=True, stop=True)
                last.then_inc(s["spread_done"], 1)

            pe.wait_ge(const_in, 16)
            pe.wait_ge(rows_in, 16 * len(ROWS))
            nc.tensor.transpose(ps[:, 5, 0:N_ROWS], rows[:, :], ident[0:N_ROWS, 0:N_ROWS])\
                .then_inc(s["rows_turned"], 1)
            for t in range(TT):
                pe.wait_ge(s["xhat_ready"], t + 1)
                for b in range(DB):
                    last = nc.tensor.transpose(xT_ps[:, b, t * P:(t + 1) * P], xhat[:, t, b * P:(b + 1) * P], ident)
            last.then_inc(s["x_turned"], 1)
            pe.wait_ge(s["cact_ready"], 1)
            ada_rows(0, 4, 0, DB)
            pe.wait_ge(s["cols_ready"], 1)
            ada_cols(0, 5)

            pe.wait_ge(s["hT_ready"], 2)
            for n in range(2):
                arrived(unit_of("w_in", n))
            for fb in range(4):
                for kk in range(DB):
                    u = unit_of("w_in", kk // 4)
                    w = slot_of(u).rearrange("p (k n) -> p k n", n=BANK)
                    last = mm(ps[:, 6 + fb // 2, (fb % 2) * SEQ:(fb % 2 + 1) * SEQ],
                              w[:, kk % 4, fb * P:(fb + 1) * P], hT[:, kk, :], start=(kk == 0), stop=(kk == DB - 1))
                if fb == 1:
                    last.then_inc(s["q_done"], 1)
            last.then_inc(unit_used, 2)

            def in_block(n):
                for t in range(TT):
                    for kk in range(DB):
                        u = unit_of("w_in", 2 * n + kk // 4)
                        arrived(u)
                        w = slot_of(u).rearrange("p (k n) -> p k n", n=BANK)
                        last = mm(ps[:, 2 * ((n - 1) % 2) + t, :], hT[:, kk, t * P:(t + 1) * P], w[:, kk % 4, :],
                                  start=(kk == 0), stop=(kk == DB - 1))
                    if t == 0:
                        last.then_inc(s["in_done"], 1)
                last.then_inc(unit_used, 2)

            in_block(1)
            in_block(2)

            def z_into(first):
                for head in range(HEADS):
                    par, b = head % 2, head // 2
                    q, kT = qkT[par * HD:par * HD + HD, b, :], qkT[par * HD:par * HD + HD, 2 + b, :]
                    mm(ps[:, 4 + par, b * SEQ:(b + 1) * SEQ], kT[:, 0:P], q, start=first, stop=True,
                       skip_group_check=not first)
                    last = mm(ps[:, 6 + par, b * P:(b + 1) * P], kT[:, P:SEQ], q[:, P:SEQ], start=first, stop=True,
                              skip_group_check=not first)
                return last

            pe.wait_ge(s["qk_ready"], 2)
            z_into(True).then_inc(s["z_done"], 1)
            pe.wait_ge(s["vu_ready"], 2)
            in_block(3)
            pe.wait_ge(s["vu_ready"], 4)
            in_block(4)
            pe.wait_ge(const_in, 32)
            pe.wait_ge(s["sp_masked"], 2)
            for par in range(2):
                mm(ps[:, 4 + par, :], k("tri_neg"), sp0[:, par], start=True, stop=True)
                mm(ps[:, 4 + par, :].rearrange("p (b q) -> p b q", b=2)[:, :, P:SEQ], k("ones_neg"), sp1[:, par],
                   start=False, stop=True, skip_group_check=True)
                mm(ps[:, 6 + par, 0:SEQ], k("tri_neg"), sp1[:, par], start=True, stop=True)
            z_into(False).then_inc(s["loga_done"], 1)
            pe.wait_ge(s["gates_ready"], 2)
            in_block(5)
            pe.wait_ge(s["a_masked"], 2)
            for head in range(HEADS):
                par, b = head % 2, head // 2
                o = ps[par * HD:par * HD + HD, 4, b * SEQ:(b + 1) * SEQ]
                mm(o, vu[:, 0, head * HD:(head + 1) * HD], a0[:, par, b, :], start=True, stop=True)
                last = mm(o[:, P:SEQ], vu[:, 1, head * HD:(head + 1) * HD], a1[:, par, b, :], start=False, stop=True,
                          skip_group_check=True)
            last.then_inc(s["o_done"], 1)
            for b in range(PB):
                for g in range(len(WINDOWS)):
                    lo, hi = max(b * P, g * GROUP), min((b + 1) * P, (g + 1) * GROUP)
                    if lo >= hi:
                        continue
                    o = ps[lo - b * P:hi - b * P, 5 + b // 2, (b % 2) * SEQ:(b % 2 + 1) * SEQ]
                    mm(o, vu[:, 0, ATTN_W + lo:ATTN_W + hi], band0[:, g, :], start=True, stop=True)
                    last = mm(o[:, P:SEQ], vu[:, 1, ATTN_W + lo:ATTN_W + hi], band1[:, g, :], start=False, stop=True,
                              skip_group_check=True)
            last.then_inc(s["mix_done"], 1)
            pe.wait_ge(s["gates_ready"], 4)
            in_block(6)
            pe.wait_ge(poolw_in, 16)
            pe.wait_ge(s["mixT_ready"], 1)

            def parts(g):
                found = []
                for b in range(PB):
                    lo, hi = max(b * P, g * GROUP), min((b + 1) * P, (g + 1) * GROUP)
                    if lo < hi:
                        found.append((b, lo - b * P, hi - b * P))
                return sorted(found, key=lambda f: f[2] - f[1])

            for g in (0, 2, 1, 3):
                if g == 1:
                    pe.wait_ge(s["even_done"], 1)
                for ob, olo, ohi in parts(g):
                    d0 = ob * P + olo - g * GROUP
                    ins = parts(g)
                    for n, (ib, ilo, ihi) in enumerate(ins):
                        last = mm(ps[olo:ohi, 5 + ob // 2, (ob % 2) * SEQ:(ob % 2 + 1) * SEQ],
                                  poolw_sb[ilo:ihi, ib, d0:d0 + ohi - olo], mixT[ilo:ihi, ib, :],
                                  start=(n == 0), stop=(n == len(ins) - 1))
                if g == 2:
                    last.then_inc(s["even_done"], 1)
            last.then_inc(s["pool_done"], 1)
            pe.wait_ge(s["gates_ready"], 8)
            pe.wait_ge(s["attnT_ready"], 1)
            arrived(unit_of("br_attn", 0))
            w = slot_of(unit_of("br_attn", 0)).rearrange("p (k n) -> p k n", n=D)
            for t in range(TT):
                for h in range(2):
                    for b in range(2):
                        last = mm(ps[:, 2 * t + h, :], attnT[:, b, t * P:(t + 1) * P],
                                  w[:, b, h * BANK:(h + 1) * BANK], start=(b == 0), stop=(b == 1))
                    if (t, h) != (1, 1):
                        last.then_inc(s["brA_done"], 1)
            last.then_inc(unit_used, 1)
            pe.wait_ge(s["poolT_ready"], 1)
            for i in range(3):
                arrived(unit_of("br_pool", i))
            for t in range(TT):
                for h in range(2):
                    for b in range(PB):
                        w = slot_of(unit_of("br_pool", b // 2)).rearrange("p (k n) -> p k n", n=D)
                        last = mm(ps[:, 4 + 2 * t + h, :], poolT[:, b, t * P:(t + 1) * P],
                                  w[:, b % 2, h * BANK:(h + 1) * BANK], start=(b == 0), stop=(b == PB - 1))
                    if (t, h) != (1, 1):
                        last.then_inc(s["brP_done"], 1)
            last.then_inc(unit_used, 3)
            pe.wait_ge(s["brA_ready"], 4)
            ada_rows(1, 0, 0, DB)
            pe.wait_ge(s["brP_ready"], 4)
            mT_ps = ps[:, 4:8, :].rearrange("p k (b t) -> p (k b) t", t=SEQ)
            for b in range(DB):
                for t in range(TT):
                    last = nc.tensor.transpose(mT_ps[:, b, t * P:(t + 1) * P], merged[:, t, b * P:(b + 1) * P], ident)
            last.then_inc(s["m_turned"], 1)
            pe.wait_ge(s["mT_ready"], 2)
            ada_cols(1, 4)
            spread_over(1, 6)
            ada_rows(2, 5, 0, DB // 2)
            pe.wait_ge(s["shift_ready"], 1)
            pe.wait_ge(router_in, 32)
            for kk in range(DB):
                mm(ps[:, 4, 0:EXPERTS], diag[:, kk, :], rw_sb[:, kk, :], start=(kk == 0), stop=False)
            mm(ps[:, 4, 0:EXPERTS], ones[0:1, :], rb_sb[0:1, :], start=False, stop=True)\
                .then_inc(s["logit0_done"], 1)
            for i in range(4):
                u = unit_of("w_out", i)
                arrived(u)
                w = slot_of(u).rearrange("p (k n) -> p k n", n=D)
                for kk in (2 * i, 2 * i + 1):
                    for t in range(TT):
                        for h in range(2):
                            last = mm(ps[:, 2 * t + h, :], hT[:, kk, t * P:(t + 1) * P],
                                      w[:, kk % 2, h * BANK:(h + 1) * BANK], start=(kk == 0), stop=(kk == DB - 1))
                last.then_inc(unit_used, 1)
            ada_rows(2, 5, DB // 2, DB)
            ada_cols(2, 4)
            for t in range(TT):
                pe.wait_ge(s["x1_ready"], t + 1)
                for b in range(DB):
                    last = nc.tensor.transpose(xT_ps[:, b, t * P:(t + 1) * P], x_sb[:, t, b * P:(b + 1) * P], ident)
            last.then_inc(s["x2_turned"], 1)
            pe.wait_ge(s["h2_ready"], 2)
            for t in range(TT):
                o = ps[:, 5, t * EXPERTS:(t + 1) * EXPERTS]
                for kk in range(DB):
                    last = mm(o, hT[:, kk, t * P:(t + 1) * P], rw_sb[:, kk, :], start=(kk == 0), stop=(kk == DB - 1))
            last.then_inc(s["logit_done"], 1)
            pe.wait_ge(s["spread_ready"], 1)
            spread_over(2, 6)
            pe.wait_ge(s["mask_ready"], 1)
            for t in range(TT):
                last = mm(ps[0:EXPERTS, 4, 0:1], mask[:, t, :], ones[:, 0:1], start=(t == 0), stop=(t == 1))
            last.then_inc(s["count_done"], 1)
            mm(ps[:, 3, 0:EXPERTS], k("before"), mask[:, 0, :], start=True, stop=True)
            mm(ps[:, 3, EXPERTS:2 * EXPERTS], k("before"), mask[:, 1, :], start=True, stop=False)
            mm(ps[:, 3, EXPERTS:2 * EXPERTS], ones, mask[:, 0, :], start=False, stop=True)\
                .then_inc(s["rank_done"], 1)
            pe.wait_ge(s["nchunk_ready"], 1)
            mm(ps[0:1, 5, 0:EXPERTS + 1], nchunk[:, 0:1], k("before_e")[0:EXPERTS, :], start=True, stop=True)
            mm(ps[0:1, 5, EXPERTS + 1:2 * EXPERTS + 1], nchunk[:, 0:1], ident[0:EXPERTS, 0:EXPERTS],
               start=True, stop=True).then_inc(s["base_done"], 1)

            def output_bias():
                pe.wait_ge(s["spread_ready"], 2)
                pe.wait_ge(s["gate_ready"], 1)
                for t in range(TT):
                    last = nc.tensor.transpose(ps[0:EXPERTS, 4, t * P:(t + 1) * P], gate[:, t, :], ident)
                last.then_inc(s["gateT_done"], 1)
                pe.wait_ge(s["gateT_ready"], 1)
                pe.wait_ge(bias_in, 32)
                for t in range(TT):
                    for h in range(2):
                        last = mm(ps[:, TURN + 2 * t + h, :], gateT[:, t * P:(t + 1) * P],
                                  bdn_sb[:, h * BANK:(h + 1) * BANK], start=True, stop=True)
                last.then_inc(s["bias_done"], 1)

            def gather(g):
                pe.wait_ge(m["pick_ready"], g + 1)
                for b in range(DB):
                    for t in range(TT):
                        last = mm(ps[:, GATHER, b * CAP:(b + 1) * CAP], x_sb[:, t, b * P:(b + 1) * P],
                                  pick[:, t, :], start=(t == 0), stop=(t == TT - 1))
                last.then_inc(m["gathered"], 1)

            def turn_pick(g):
                for t in range(TT):
                    last = nc.tensor.transpose(ps[:, DOWN, t * P:(t + 1) * P], pickg[:, t, :], ident)
                last.then_inc(m["pick_turned"], 1)

            def scatter(g):
                ge(pe, m["ye_ready"], g)
                ge(pe, m["pickT_ready"], g)
                for t in range(TT):
                    for h in range(2):
                        last = mm(ps[:, TURN + 2 * t + h, :], pickT[CAP * h:CAP * h + CAP, t * P:(t + 1) * P],
                                  ye[CAP * h:CAP * h + CAP, :], start=True, stop=True)
                last.then_inc(m["scattered"], 1)

            def down(g, e, release):
                pe.wait_ge(m["act_ready"], g)
                pe.wait_ge(m["acc_ready"], g)
                for j in range(4):
                    last = nc.tensor.transpose(ps[:, TURN, j * P:(j + 1) * P], act_sb[:, j * P:(j + 1) * P], ident)
                    if release and j == 0:
                        last.then_inc(unit_used, 1)
                last.then_inc(m["turned"], 1)
                pe.wait_ge(m["actT_ready"], g)
                arrivals = list(expert_units(GU_UNITS, DN_UNITS, e))
                for fb in range(DB):
                    at, count = arrivals[fb // 2]
                    if fb % 2 == 0:
                        pe.wait_ge(unit_in[at], count)
                    w = ring[:, at, :].rearrange("p (k n) -> p k n", n=D)
                    lhs = actT[:, fb % 4, (fb // 4) * CAP:(fb // 4 + 1) * CAP]
                    for h in range(2):
                        last = mm(ps[CAP * h:CAP * h + CAP, DOWN, :], lhs, w[:, fb % 2, h * BANK:(h + 1) * BANK],
                                  start=(fb == 0), stop=(fb == DB - 1))
                        if release and fb and fb % 2 == 0 and h == 0:
                            last.then_inc(unit_used, 1)
                last.then_inc(m["down_done"], 1)

            def gate_up(g, e, release, release_before, first=False):
                outs = [(ps[CAP * h:CAP * h + CAP, bank, :], (2 * bank + h) * BANK)
                        for bank in (GATE, UP) for h in range(2)]
                if first:
                    pe.wait_ge(bias_in, 32)
                for n, (o, c0) in enumerate(outs):
                    last = mm(o, esel[:, :], bgu_sb[:, c0:c0 + BANK], start=True, stop=False)
                    if release_before and n == 0:
                        last.then_inc(unit_used, 1)
                pe.wait_ge(m["xg_ready"], g + 1)
                for kk, (at, count) in enumerate(expert_units(0, GU_UNITS, e)):
                    pe.wait_ge(unit_in[at], count)
                    for n, (o, c0) in enumerate(outs):
                        last = mm(o, xg[:, kk, :], ring[:, at, c0:c0 + BANK], start=False, stop=(kk == DB - 1))
                        if release and kk and n == 0:
                            last.then_inc(unit_used, 1)
                    if kk == 1:
                        if not first:
                            scatter(g)
                        turn_pick(g)
                last.then_inc(m["gu_done"], 1)

            def chunk(g, e, e_before, last, last_before):
                gather(g)
                down(g, e_before, last_before)
                gate_up(g, e, last, last_before)

            def first_chunk(last):
                gather(0)
                gate_up(0, 0, last, False, first=True)
                output_bias()

            def expert(e, start):
                n = pe.value_load(base[0:1, bass.ds(e + EXPERTS + 1, 1)], min_val=1, max_val=CHUNKS)
                b0 = pe.value_load(base[0:1, bass.ds(e, 1)], min_val=0, max_val=MAX_CHUNKS)
                with pe.If(n > 1):
                    start(b0, False)
                    with pe.If(n > 2):
                        with pe.Fori(1, n - 1) as c:
                            chunk(b0 + c, e, e, False, False)
                    final = pe.value_load(base[0:1, bass.ds(e + 2 * EXPERTS + 1, 1)], min_val=1,
                                          max_val=MAX_CHUNKS)
                    chunk(final, e, e, True, False)
                with pe.Else():
                    start(b0, True)

            pe.wait_ge(s["base_ready"], 2)
            expert(0, lambda b0, last: first_chunk(last))
            with pe.Fori(1, EXPERTS) as e:
                expert(e, lambda b0, last: chunk(b0, e, e - 1, last, True))
            n = pe.value_load(base[0:1, EXPERTS:EXPERTS + 1], min_val=EXPERTS, max_val=MAX_CHUNKS)
            down(n, EXPERTS - 1, False)
            scatter(n)

        @block.scalar
        def _(act):
            A = nc.scalar.activation
            steps = [0]

            def link(ins):
                steps[0] += 1
                ins.then_inc(s["act_step"], 1)
                act.wait_ge(s["act_step"], steps[0])

            for name, src in (("ada_b", ada_b), ("pre1_g", pre1_g), ("post1_g", post1_g), ("pre2_g", pre2_g),
                              ("post2_g", post2_g), ("c", c)):
                lo, hi = ROWS[name]
                act.dma_start(rows[lo:hi, :], src[0].rearrange("(r p) -> r p", p=P)).then_inc(rows_in, 16)
            for name, src in (("pool_b", pool_b), ("pool_scale", pool_scale)):
                lo, hi = ROWS[name]
                act.dma_start(rows[lo:hi, :], src[0].rearrange("g n -> (g n)").rearrange("(r p) -> r p", p=P))\
                    .then_inc(rows_in, 16)

            tables = [-1]

            def load_table(func):
                tables[0] += 1
                A(unread[:, tables[0]:tables[0] + 1], ident[:, 0:1], func)

            def small_loads():
                act.dma_start(const[:, CONST_FIRST:CONST_W], consts[:, CONST_FIRST:CONST_W]).then_inc(const_in, 16)
                act.dma_start(poolw_sb[:, :, :], pool_w[0].rearrange("g n d -> (g n) d")
                              .rearrange("(b p) d -> p b d", p=P)).then_inc(poolw_in, 16)
                act.dma_start(rw_sb[:, :, :], router_w[0].rearrange("(k p) e -> p k e", p=P)).then_inc(router_in, 16)
                act.dma_start(rb_sb[:, :], router_b).then_inc(router_in, 16)
                act.dma_start(bgu_sb[:, :], b_gu[0]).then_inc(bias_in, 16)
                act.dma_start(bdn_sb[:, :], b_dn[0]).then_inc(bias_in, 16)

            def square_sums(src, at, done):
                for t in range(TT):
                    link(A(junk, src[:, t, :], ACT.Square, accum_out=stat[:, at + t:at + t + 1]))
                nc.scalar.activation(stat[:, 12:13], stat[:, at:at + 1], ACT.Copy).then_inc(s[done], 1)

            def std(n, at):
                act.wait_ge(s["var_ready"], n)
                A(stat[:, at:at + TT], stat[:, at:at + TT], ACT.Sqrt).then_inc(s["std_ready"], 1)

            def normed(n, at, src, dst, done):
                act.wait_ge(s["rstd_ready"], n)
                for t in range(TT):
                    A(dst[:, t, :], src[:, t, :], ACT.Copy, scale=stat[:, at + t:at + t + 1]).then_inc(s[done], 1)

            act.wait_ge(const_in, 16)
            load_table(ACT.Sqrt)
            act.wait_ge(x_in, 16)
            square_sums(x_sb, 0, "squares_ready")
            std(1, 0)
            normed(1, 0, x_sb, xhat, "xhat_ready")
            act.wait_ge(s["cols_ready"], 1)
            A(csig[:, :], col("c"), ACT.Sigmoid).then_inc(s["csig_ready"], 1)
            small_loads()

            def affine(n, f, shift, done):
                for b in range(4, DB):
                    last = A(hT[:, b, :], xT_ps[:, b, :], ACT.Identity, scale=fac[:, f, b:b + 1],
                             bias=mod[:, shift + b:shift + b + 1])
                last.then_inc(s[done], 1)

            act.wait_ge(s["x_turned"], 1)
            act.wait_ge(s["mod_ready"], 1)
            affine(1, 0, 0, "hT_ready")
            for n, scale in ((0, HD ** -0.5), (1, 1.0)):
                if n == 0:
                    act.wait_ge(s["q_done"], 1)
                else:
                    used(act, "w_in", 1)
                A(qkT[:, 2 * n:2 * n + 2, :], ps[:, 6 + n, :].rearrange("p (b t) -> p b t", t=SEQ), ACT.Copy,
                  scale=scale).then_inc(s["qk_ready"], 1)
            z0, z1 = ps[:, 4:6, :], ps[:, 6:8, 0:SEQ]
            e0v, e1v = e0.rearrange("p (a n) -> p a n", a=2), e1.rearrange("p (a n) -> p a n", a=2)
            act.wait_ge(s["z_done"], 1)
            A(e0v, z0, ACT.Abs).then_inc(s["act_step"], 1)
            A(e1v, z1, ACT.Abs).then_inc(s["act_step"], 1)
            steps[0] += 2
            act.wait_ge(s["act_step"], steps[0])
            for func, scale, bias in ((ACT.Exp, -1.0, 0.0), (ACT.Ln, 1.0, 1.0)):
                link(A(area2[:, 1536:3072], area2[:, 1536:3072], func, scale=scale, bias=bias))
            A(stat[:, 13:14], stat[:, 0:1], ACT.Copy).then_inc(s["sp_part"], 1)

            def gate_block(n):
                for t in range(TT):
                    in_block_done(act, n, t)
                    A(gates[:, t, (n - 3) * BANK:(n - 2) * BANK], ps[:, 2 * ((n - 1) % 2) + t, :], ACT.Sigmoid)\
                        .then_inc(s["gates_ready"], 1)

            gate_block(3)
            gate_block(4)
            act.wait_ge(s["loga_done"], 1)
            A(a0, z0.rearrange("p a (b q) -> p a b q", b=2), ACT.Exp).then_inc(s["a_ready"], 1)
            A(a1, z1.rearrange("p a (b q) -> p a b q", b=2), ACT.Exp).then_inc(s["a_ready"], 1)
            gate_block(5)
            act.wait_ge(s["o_done"], 1)
            A(attnT[:, :, :], ps[:, 4, :].rearrange("p (b t) -> p b t", t=SEQ), ACT.Copy)\
                .then_inc(s["attnT_ready"], 1)
            gate_block(6)
            act.wait_ge(s["m_turned"], 1)
            for n in range(2):
                last = A(hT[:, 4 + 2 * n:6 + 2 * n, :], ps[:, 6 + n, :].rearrange("p (b t) -> p b t", t=SEQ), ACT.Copy)
            last.then_inc(s["mT_ready"], 1)
            load_table(ACT.Sqrt)
            y_ps = ps[:, 0:4, :].rearrange("p (t h) n -> p t (h n)", t=TT)
            used(act, "w_out", 3)
            A(junk, y_ps[:, 0, :], ACT.Square, accum_out=stat[:, 2:3]).then_inc(s["y0_squared"], 1)
            act.wait_ge(s["y1_spread"], 1)
            act.wait_ge(s["y0_squared"], 1)
            link(A(junk, y_ps[:, 1, :], ACT.Square, accum_out=stat[:, 3:4]))
            A(stat[:, 12:13], stat[:, 2:3], ACT.Copy).then_inc(s["squares_ready"], 1)
            std(2, 2)
            used(act, "ada2", DB - 1)
            A(modrow[:, :], ps[:, 5, :], ACT.Copy).then_inc(s["modrow_ready"], 1)
            for t in range(TT):
                act.wait_ge(s["x1_ready"], t + 1)
                link(A(junk, x_sb[:, t, :], ACT.Square, accum_out=stat[:, 4 + t:5 + t]))
            A(stat[:, 12:13], stat[:, 4:5], ACT.Copy).then_inc(s["squares_ready"], 1)
            std(3, 4)
            act.wait_ge(s["x2_turned"], 1)
            A(hT[:, 4:8, :], xT_ps[:, 4:8, :], ACT.Copy).then_inc(s["h2_ready"], 1)
            load_table(ACT.Exp)
            act.wait_ge(s["spread_done"], 2)
            A(spread[:, :].rearrange("p (h n) -> p h n", h=2), ps[:, 6:8, :], ACT.Copy)\
                .then_inc(s["spread_ready"], 1)
            act.wait_ge(s["logit_ready"], 1)
            A(top_e[:, :, :], top_f[:, :, :], ACT.Exp).then_inc(s["exp_ready"], 1)
            load_table(ACT.Sigmoid)

            def back(g, end=False):
                act.wait_ge(m["gmin_ready"], g)
                A(g_sig, g_min, ACT.Sigmoid, scale=ALPHA).then_inc(m["sig_ready"], 1)
                act.wait_ge(m["turned"], g)
                A(actT, ps[:, TURN, :].rearrange("p (j s) -> p j s", s=P), ACT.Copy).then_inc(m["actT_ready"], 1)
                if end:
                    load_table(ACT.Sqrt)
                act.wait_ge(m["down_done"], g)
                A(ye, ps[:, DOWN, :], ACT.Copy).then_inc(m["ye_ready"], 1)

            def front(g):
                act.wait_ge(m["pick_turned"], g + 1)
                A(pickT, ps[:, DOWN, 0:2 * P], ACT.Copy).then_inc(m["pickT_ready"], 1)

            act.wait_ge(s["base_ready"], 2)

            def more_chunks(e):
                b0 = act.value_load(base[0:1, bass.ds(e, 1)], min_val=0, max_val=MAX_CHUNKS)
                n = act.value_load(base[0:1, bass.ds(e + EXPERTS + 1, 1)], min_val=1, max_val=CHUNKS)
                with act.If(n > 1):
                    with act.Fori(1, n) as c:
                        back(b0 + c)
                        front(b0 + c)

            front(0)
            act.wait_ge(s["gateT_done"], 1)
            A(gateT[:, :], ps[0:EXPERTS, 4, 0:SEQ], ACT.Copy).then_inc(s["gateT_ready"], 1)
            act.wait_ge(s["bias_done"], 1)
            A(yacc[:, :, :], ps[:, TURN:8, :].rearrange("p (t h) n -> p t (h n)", t=TT), ACT.Copy)\
                .then_inc(m["acc_ready"], 1)
            more_chunks(0)
            with act.Fori(1, EXPERTS) as e:
                b0 = act.value_load(base[0:1, bass.ds(e, 1)], min_val=1, max_val=MAX_CHUNKS)
                back(b0)
                front(b0)
                more_chunks(e)
            n = act.value_load(base[0:1, EXPERTS:EXPERTS + 1], min_val=EXPERTS, max_val=MAX_CHUNKS)
            back(n, end=True)
            for t in range(TT):
                act.wait_ge(s["ysum_ready"], t + 1)
                link(A(junk, yacc[:, t, :], ACT.Square, accum_out=stat[:, 6 + t:7 + t]))
            A(stat[:, 12:13], stat[:, 6:7], ACT.Copy).then_inc(s["squares_ready"], 1)
            std(4, 6)

        @block.gpsimd
        def _(pool):
            def causal(tile, width, done):
                nc.gpsimd.affine_select(out=tile, in_=tile, compare_op=ALU.is_gt, fill=0.0, base=0,
                                        pattern=[[0, 2], [0, 2], [1, width]], channel_multiplier=-1).then_inc(done, 1)

            pool.wait_ge(s["sp_ready"], 2)
            causal(sp0, SEQ, s["sp_masked"])
            causal(sp1, P, s["sp_masked"])
            pool.wait_ge(s["a_ready"], 2)
            causal(a0, SEQ, s["a_masked"])
            causal(a1, P, s["a_masked"])

        @block.vector
        def _(dve):
            V = nc.vector
            steps = [0]

            def link(ins):
                steps[0] += 1
                ins.then_inc(s["dve_step"], 1)
                dve.wait_ge(s["dve_step"], steps[0])

            def variance(n, at):
                dve.wait_ge(s["squares_ready"], n)
                V.tensor_scalar(stat[:, at:at + TT], stat[:, at:at + TT], 1.0 / D, EPS, ALU.mult, ALU.add)\
                    .then_inc(s["var_ready"], 1)

            def rstd(n, at, done=True):
                dve.wait_ge(s["std_ready"], n)
                ins = V.reciprocal(stat[:, at:at + TT], stat[:, at:at + TT])
                if done:
                    ins.then_inc(s["rstd_ready"], 1)
                else:
                    link(ins)

            def over(ap, n):
                return ap.unsqueeze(2).broadcast_to([ap.shape[0], ap.shape[1], n])

            dve.wait_ge(s["rows_turned"], 1)
            V.tensor_copy(cols[:, :], ps[:, 5, 0:N_ROWS]).then_inc(s["cols_ready"], 1)
            variance(1, 0)
            rstd(1, 0)
            dve.wait_ge(s["csig_ready"], 1)
            dve.wait_ge(s["cols_ready"], 1)
            V.tensor_tensor(cact[:, :, :], over(col("c"), 32), over(csig[:, :], 32), ALU.mult)\
                .then_inc(s["cact_ready"], 1)

            def mod_rows(j, bank):
                used(dve, f"ada{j}", DB - 1)
                V.tensor_copy(modrow[:, :], ps[:, bank, :]).then_inc(s["modrow_ready"], 1)

            def mod_cols(j, bank):
                dve.wait_ge(s["modcol_done"], j + 1)
                link(V.tensor_tensor(mod[:, 16 * j:16 * j + 16], ps[:, bank, 0:16], col("ada_b", 16 * j, 16 * j + 16),
                                     ALU.add))

            def factor(f, at, gain, plus):
                return V.scalar_tensor_tensor(out=fac[:, f, :], in0=mod[:, at:at + DB], scalar=plus, in1=col(gain),
                                              op0=ALU.add, op1=ALU.mult)

            def affine(f, shift, done):
                for b in range(4):
                    last = V.tensor_scalar(hT[:, b, :], xT_ps[:, b, :], fac[:, f, b:b + 1],
                                           mod[:, shift + b:shift + b + 1], ALU.mult, ALU.add)
                last.then_inc(s[done], 1)

            mod_rows(0, 4)
            mod_cols(0, 5)
            link(factor(0, DB, "pre1_g", 1.0))
            V.tensor_copy(stat[:, 14:15], stat[:, 0:1]).then_inc(s["mod_ready"], 1)
            dve.wait_ge(s["x_turned"], 1)
            affine(0, 0, "hT_ready")
            for n in (1, 2):
                for t in range(TT):
                    in_block_done(dve, n, t)
                    V.tensor_copy(vu[:, t, (n - 1) * BANK:n * BANK], ps[:, 2 * (n - 1) + t, :])\
                        .then_inc(s["vu_ready"], 1)
            z0, z1 = ps[:, 4:6, :], ps[:, 6:8, 0:SEQ]
            dve.wait_ge(s["sp_part"], 1)
            V.scalar_tensor_tensor(out=area2[:, 0:1024].rearrange("p (a n) -> p a n", a=2), in0=z0, scalar=0.0,
                                   in1=e0.rearrange("p (a n) -> p a n", a=2), op0=ALU.max, op1=ALU.add)\
                .then_inc(s["sp_ready"], 1)
            V.scalar_tensor_tensor(out=area2[:, 1024:1536].rearrange("p (a n) -> p a n", a=2), in0=z1, scalar=0.0,
                                   in1=e1.rearrange("p (a n) -> p a n", a=2), op0=ALU.max, op1=ALU.add)\
                .then_inc(s["sp_ready"], 1)
            dve.wait_ge(s["mix_done"], 1)
            V.tensor_copy(mixT, ps[:, 5:8, :].rearrange("p k (b t) -> p (k b) t", t=SEQ)).then_inc(s["mixT_ready"], 1)
            dve.wait_ge(s["pool_done"], 1)
            for b in range(PB):
                last = V.tensor_scalar(poolT[:, b, :], ps[:, 5 + b // 2, (b % 2) * SEQ:(b % 2 + 1) * SEQ],
                                       col("pool_b", b, b + 1), col("pool_scale", b, b + 1), ALU.add, ALU.mult)
            last.then_inc(s["poolT_ready"], 1)
            for t in range(TT):
                for h in range(2):
                    branch_done(dve, s["brA_done"], "br_attn", 0, t, h)
                    V.tensor_tensor(merged[:, t, h * BANK:(h + 1) * BANK], ps[:, 2 * t + h, :],
                                    gates[:, t, h * BANK:(h + 1) * BANK], ALU.mult).then_inc(s["brA_ready"], 1)
            for t in range(TT):
                for h in range(2):
                    branch_done(dve, s["brP_done"], "br_pool", 2, t, h)
                    link(V.tensor_tensor(prod[:, h, :], ps[:, 4 + 2 * t + h, :],
                                         gates[:, t, D + h * BANK:D + (h + 1) * BANK], ALU.mult))
                    half = merged[:, t, h * BANK:(h + 1) * BANK]
                    V.tensor_tensor(half, half, prod[:, h, :], ALU.add).then_inc(s["brP_ready"], 1)
            mod_rows(1, 0)
            dve.wait_ge(s["m_turned"], 1)
            V.tensor_copy(hT[:, 0:4, :], ps[:, 4:6, :].rearrange("p k (b t) -> p (k b) t", t=SEQ))\
                .then_inc(s["mT_ready"], 1)
            mod_cols(1, 4)
            link(factor(1, 2 * DB, "post1_g", 0.0))
            V.tensor_copy(stat[:, 14:15], stat[:, 0:1]).then_inc(s["mod_ready"], 1)

            def diagonal(f):
                V.tensor_tensor(diag, ident.unsqueeze(1).broadcast_to([P, DB, P]), over(fac[:, f, :], P), ALU.mult)\
                    .then_inc(s["diag_ready"], 1)

            def spread_read(n, bank):
                dve.wait_ge(s["spread_done"], n)
                ins = V.tensor_copy(spread[:, :].rearrange("p (h n) -> p h n", h=2), ps[:, bank:bank + 2, :])
                ins.then_inc(s["spread_ready"], 1)

            diagonal(1)
            spread_read(1, 6)
            V.tensor_copy(diag, over(mod[:, 3 * DB:4 * DB], P)).then_inc(s["shift_ready"], 1)
            dve.wait_ge(s["logit0_done"], 1)
            V.tensor_copy(logit0[:, :], ps[:, 4, 0:EXPERTS]).then_inc(s["logit0_ready"], 1)
            y_ps = ps[:, 0:4, :].rearrange("p (t h) n -> p t (h n)", t=TT)
            dve.wait_ge(s["spread_ready"], 1)
            used(dve, "w_out", 3)
            V.tensor_tensor(yspread[:, 1, :], y_ps[:, 1, :], spread[:, :], ALU.mult).then_inc(s["y1_spread"], 1)
            dve.wait_ge(s["y0_squared"], 1)
            link(V.tensor_tensor(yspread[:, 0, :], y_ps[:, 0, :], spread[:, :], ALU.mult))
            variance(2, 2)
            rstd(2, 2, done=False)
            dve.wait_ge(s["y1_spread"], 1)
            for t in range(TT):
                V.scalar_tensor_tensor(out=x_sb[:, t, :], in0=yspread[:, t, :], scalar=stat[:, 2 + t:3 + t],
                                       in1=x_sb[:, t, :], op0=ALU.mult, op1=ALU.add).then_inc(s["x1_ready"], 1)
            mod_cols(2, 4)
            link(factor(2, 4 * DB, "pre2_g", 1.0))
            dve.wait_ge(s["logit0_ready"], 1)
            link(V.tensor_tensor(rw_sb[:, :, :], rw_sb[:, :, :], over(fac[:, 2, :], EXPERTS), ALU.mult))
            variance(3, 4)
            dve.wait_ge(s["x2_turned"], 1)
            V.tensor_copy(hT[:, 0:4, :], xT_ps[:, 0:4, :]).then_inc(s["h2_ready"], 1)
            rstd(3, 4, done=False)
            link(factor(3, 5 * DB, "post2_g", 0.0))
            diagonal(3)
            dve.wait_ge(s["logit_done"], 1)
            for t in range(TT):
                V.scalar_tensor_tensor(out=logit[:, t, :], in0=ps[:, 5, t * EXPERTS:(t + 1) * EXPERTS],
                                       scalar=stat[:, 4 + t:5 + t], in1=logit0[:, :], op0=ALU.mult, op1=ALU.add)\
                    .then_inc(s["logits_here"], 1)
            for t in range(TT):
                dve.wait_ge(s["logits_here"], t + 1)
                V.max(top_v[:, t, :], logit[:, t, :]).then_inc(s["max_here"], 1)
            for t in range(TT):
                dve.wait_ge(s["max_here"], t + 1)
                last = V.max_index(top_i[:, t, :], top_v[:, t, :], logit[:, t, :])
            link(last)
            link(V.tensor_copy(top_g[:, :, :], top_i[:, :, 0:TOP_K]))
            for t in range(TT):
                last = V.tensor_tensor(hot[:, t], k("expert").unsqueeze(1).broadcast_to([P, TOP_K, EXPERTS]),
                                       over(top_g[:, t, :], EXPERTS), ALU.is_equal)
            link(last)
            for t in range(TT):
                last = V.tensor_reduce(mask[:, t, :], hot[:, t].rearrange("p r e -> p e r"), AX.X, ALU.add)
            last.then_inc(s["mask_ready"], 1)
            for t in range(TT):
                last = V.tensor_scalar(top_f[:, t, :], top_v[:, t, 0:TOP_K], top_v[:, t, 0:1], None, ALU.subtract)
            last.then_inc(s["logit_ready"], 1)
            dve.wait_ge(s["count_done"], 1)
            V.tensor_scalar(nchunk[:, 1:CHUNKS], k("passed")[0:EXPERTS, :], ps[0:EXPERTS, 4, 0:1], 1.0, ALU.is_lt,
                            ALU.add, accum_out=nchunk[:, 0:1]).then_inc(s["nchunk_ready"], 1)
            dve.wait_ge(s["rank_done"], 1)
            dve.wait_ge(s["mask_ready"], 1)
            V.scalar_tensor_tensor(out=rank[:, :, :], in0=ps[:, 3, 0:TT * EXPERTS]
                                   .rearrange("p (t e) -> p t e", t=TT), scalar=1.0, in1=mask[:, :, :],
                                   op0=ALU.add, op1=ALU.mult).then_inc(s["rank_ready"], 1)
            dve.wait_ge(s["base_done"], 1)
            V.tensor_copy(base[:, 0:2 * EXPERTS + 1], ps[0:1, 5, 0:2 * EXPERTS + 1]).then_inc(s["base_ready"], 1)
            V.tensor_scalar(base[:, 2 * EXPERTS + 1:3 * EXPERTS + 1], ps[0:1, 5, 1:EXPERTS + 1], -1.0, None, ALU.add)\
                .then_inc(s["base_ready"], 1)
            dve.wait_ge(s["exp_ready"], 1)
            for t in range(TT):
                last = V.tensor_reduce(stat[:, 8 + t:9 + t], top_e[:, t, :], AX.X, ALU.add)
            link(last)
            link(V.reciprocal(stat[:, 8:8 + TT], stat[:, 8:8 + TT]))
            for t in range(TT):
                last = V.tensor_scalar(top_e[:, t, :], top_e[:, t, :], stat[:, 8 + t:9 + t], None, ALU.mult)
            link(last)
            for t in range(TT):
                last = V.tensor_tensor(hotg[:, t], hot[:, t], over(top_e[:, t, :], EXPERTS), ALU.mult)
            link(last)
            for t in range(TT):
                last = V.tensor_reduce(gate[:, t, :], hotg[:, t].rearrange("p r e -> p e r"), AX.X, ALU.add)
            last.then_inc(s["gate_ready"], 1)
            dve.wait_ge(s["rank_ready"], 1)
            dve.wait_ge(s["base_ready"], 2)
            dve.wait_ge(s["gate_ready"], 1)

            def picks(g, e, c):
                ge(dve, m["pick_turned"], g)
                for t in range(TT):
                    r = rank[:, t, bass.ds(e, 1)]
                    V.tensor_scalar(pick[:, t, :], slot[:, bass.ds(c, 1), 0:CAP].rearrange("p o s -> p (o s)"),
                                    r, stat[:, 4 + t:5 + t], ALU.is_equal, ALU.mult)
                    if t == 0:
                        V.tensor_copy(esel[:, :], ident[0:EXPERTS, bass.ds(e, 1)].broadcast_to([EXPERTS, CAP]))
                    last = V.tensor_scalar(pickg[:, t, :], slot[:, bass.ds(c, 1), :].rearrange("p o s -> p (o s)"),
                                           r, gate[:, t, bass.ds(e, 1)], ALU.is_equal, ALU.mult)
                last.then_inc(m["pick_ready"], 1)

            def activate(g):
                dve.wait_ge(m["gu_done"], g)
                V.tensor_scalar(g_min, ps[:, GATE, :], LIMIT, None, ALU.min).then_inc(m["gmin_ready"], 1)
                V.tensor_scalar(u_clip, ps[:, UP, :], LIMIT, -LIMIT, ALU.min, ALU.max).then_inc(m["u_ready"], 1)
                dve.wait_ge(m["sig_ready"], g)
                V.tensor_tensor(g_act, g_min, g_sig, ALU.mult).then_inc(m["gact_ready"], 1)
                dve.wait_ge(m["gact_ready"], g)
                dve.wait_ge(m["u_ready"], g)
                V.scalar_tensor_tensor(out=act_sb, in0=u_clip, scalar=1.0, in1=g_act, op0=ALU.add, op1=ALU.mult)\
                    .then_inc(m["act_ready"], 1)

            def affine_gathered(g):
                dve.wait_ge(m["gathered"], g + 1)
                V.tensor_tensor(xg_m, ps[:, GATHER, :].rearrange("p (b s) -> p b s", s=CAP),
                                over(fac[:, 2, :], CAP), ALU.mult).then_inc(m["xgm_ready"], 1)
                dve.wait_ge(m["xgm_ready"], g + 1)
                V.tensor_tensor(xg, xg_m, over(mod[:, 3 * DB:4 * DB], CAP), ALU.add).then_inc(m["xg_ready"], 1)

            def accumulate(g):
                dve.wait_ge(m["scattered"], g)
                dve.wait_ge(m["acc_ready"], g)
                V.tensor_tensor(yacc[:, :, :], yacc[:, :, :],
                                ps[:, TURN:8, :].rearrange("p (t h) n -> p t (h n)", t=TT), ALU.add)\
                    .then_inc(m["acc_ready"], 1)

            def more_chunks(e):
                b0 = dve.value_load(base[0:1, bass.ds(e, 1)], min_val=0, max_val=MAX_CHUNKS)
                n = dve.value_load(base[0:1, bass.ds(e + EXPERTS + 1, 1)], min_val=1, max_val=CHUNKS)
                with dve.If(n > 1):
                    with dve.Fori(1, n) as c:
                        picks(b0 + c, e, c)
                        activate(b0 + c)
                        affine_gathered(b0 + c)
                        accumulate(b0 + c)

            picks(0, 0, 0)
            affine_gathered(0)
            more_chunks(0)
            with dve.Fori(1, EXPERTS) as e:
                b0 = dve.value_load(base[0:1, bass.ds(e, 1)], min_val=1, max_val=MAX_CHUNKS)
                picks(b0, e, 0)
                activate(b0)
                affine_gathered(b0)
                accumulate(b0)
                more_chunks(e)
            n = dve.value_load(base[0:1, EXPERTS:EXPERTS + 1], min_val=EXPERTS, max_val=MAX_CHUNKS)
            activate(n)
            dve.wait_ge(m["scattered"], n)
            dve.wait_ge(m["acc_ready"], n)
            for t in range(TT):
                V.tensor_tensor(yacc[:, t, :], yacc[:, t, :],
                                ps[:, TURN + 2 * t:TURN + 2 * t + 2, :].rearrange("p h n -> p (h n)"), ALU.add)\
                    .then_inc(s["ysum_ready"], 1)
            dve.wait_ge(s["spread_ready"], 2)
            for t in range(TT):
                dve.wait_ge(s["ysum_ready"], t + 1)
                link(V.tensor_tensor(yspread[:, t, :], yacc[:, t, :], spread[:, :], ALU.mult))
            variance(4, 6)
            rstd(4, 6, done=False)
            for t in range(TT):
                V.scalar_tensor_tensor(out=tail[:, t, :], in0=yspread[:, t, :], scalar=stat[:, 6 + t:7 + t],
                                       in1=x_sb[:, t, :], op0=ALU.mult, op1=ALU.add).then_inc(s["out_done"], 1)


_INS = ["x", "c", "ada_w", "ada_b", "pre1_g", "post1_g", "pre2_g", "post2_g", "w_in", "pool_w", "pool_b",
        "pool_scale", "w_br_attn", "w_br_pool", "w_out", "router_w", "router_b", "w_gu", "b_gu", "w_dn", "b_dn"]


def constants(np):
    v = np.zeros((P, CONST_W), np.float32)
    row, colm = np.arange(P)[:, None], np.arange(P)[None, :]

    def put(name, value):
        a, b = CONSTS[name]
        v[:, a:b] = value

    put("ident", row == colm)
    put("tri_neg", np.where(row >= colm, -1.0, 0.0))
    put("ones_neg", -1.0)
    put("before", row < colm)
    put("ones", 1.0)
    tok, query = np.arange(SEQ)[:, None], np.arange(SEQ)[None, :]
    bands = []
    for w in WINDOWS:
        inside = (query - tok >= 0) & (query - tok < w)
        bands.append(np.where(inside, 1.0 / np.minimum(query + 1, w), 0.0) - (query == tok))
    put("band0", np.concatenate([b[0:P] for b in bands], axis=1))
    put("band1", np.concatenate([b[P:SEQ, P:SEQ] for b in bands], axis=1))
    put("slot", np.concatenate([CAP * n + 1 + np.arange(P) % CAP for n in range(CHUNKS)])[None, :])
    put("passed", CAP * np.arange(1, CHUNKS)[None, :])
    put("expert", np.arange(EXPERTS)[None, :])
    put("before_e", row < np.arange(EXPERTS + 1)[None, :])
    put("quad", row == 32 * np.arange(4)[None, :])
    return v


def kernel(**inputs):
    import numpy as np
    import concourse.bacc as bacc
    from concourse.bass_utils import run_bass_kernel_spmd

    nc = bacc.Bacc("TRN2", target_bir_lowering=False, num_devices=1)
    arrays, args = {}, []
    for name in _INS:
        a = np.ascontiguousarray(inputs[name])
        arrays[f"in_{name}"] = a
        args.append(nc.dram_tensor(f"in_{name}", a.shape, mybir.dt.from_np(a.dtype), kind="ExternalInput").ap())
    table = constants(np)
    arrays["in_consts"] = table
    args.append(nc.dram_tensor("in_consts", table.shape, mybir.dt.float32, kind="ExternalInput").ap())
    args.append(nc.dram_tensor("out_0", (1, SEQ, D), mybir.dt.float32, kind="ExternalOutput").ap())
    build(nc, *args)
    r = run_bass_kernel_spmd(nc, [arrays], core_ids=[0])
    return r.results[0]["out_0"]
```

```python
import concourse.bass as bass
from concourse import mybir
from contextlib import ExitStack
import math

P = 128
SEQ, D = 256, 1024
TT = SEQ // P
DB = D // P
BANK = 512
HEADS, HD = 4, 64
ATTN_W = HEADS * HD
POOL_W = D - ATTN_W
WINDOWS = (2, 4, 8, 16)
GROUP = POOL_W // len(WINDOWS)
PB = POOL_W // P
IN_W = 3 * ATTN_W + POOL_W + 2 * D
EXPERTS, TOP_K = 32, 4
F = D
CAP = 64
CHUNKS = SEQ // CAP
MAX_CHUNKS = EXPERTS + SEQ * TOP_K // CAP
LIMIT, ALPHA, EPS = 7.0, 1.702, 1e-6

CONSTS = {}
_at = 0
for _name, _width in (("ident", P), ("ones", P), ("quad", 4), ("tri_neg", P), ("ones_neg", P),
                      ("band0", len(WINDOWS) * SEQ), ("band1", len(WINDOWS) * P), ("before", P),
                      ("slot", CHUNKS * P), ("expert", EXPERTS), ("row_of", EXPERTS), ("before_e", EXPERTS + 1), ("passed", CHUNKS - 1)):
    CONSTS[_name] = (_at, _at + _width)
    _at += _width
CONST_W = _at
N_BANDS = CONSTS["band1"][1] - CONSTS["tri_neg"][0]
CONST_FIRST = CONSTS["quad"][1]

ROWS = {}
_at = 0
for _name, _count in (("ada_b", 6 * DB), ("pre1_g", DB), ("post1_g", DB), ("pre2_g", DB),
                      ("post2_g", DB), ("c", DB), ("pool_b", PB), ("pool_scale", PB)):
    ROWS[_name] = (_at, _at + _count)
    _at += _count
N_ROWS = _at

RING, LATE, EXTRA, SLOT_W = 7, 5, 4, 2048
SLOTS = RING + LATE + EXTRA
POOL_ADA = [(f"ada{j}", k) for j in (1, 2) for k in range(DB)]
MIX_UNITS = [("ada0", k) for k in range(DB)] + [("w_in", i) for i in range(2)]
_weights = ([("w_in", i) for i in range(2, 2 * IN_W // BANK)] + [("br_attn", 0)]
            + [("br_pool", i) for i in range(3)] + [("w_out", i) for i in range(4)])
for _i, _unit in enumerate(_weights):
    MIX_UNITS += [_unit] + POOL_ADA[_i:_i + 1]
N_MIX = len(MIX_UNITS)
GU_UNITS, DN_UNITS = DB, 4
UNITS = GU_UNITS + DN_UNITS
assert UNITS == RING + LATE
ROUND = SLOTS // math.gcd(UNITS, SLOTS)
TURNS = UNITS // math.gcd(UNITS, SLOTS)
assert EXPERTS % ROUND == 0

SPLIT_UNITS = [u for u, (name, _) in enumerate(MIX_UNITS) if name in ("w_in", "br_pool", "w_out")]
PARTS, PART_W, PAIRS = 2 * len(SPLIT_UNITS), SLOT_W // 2, 3
POOL_UNITS = [MIX_UNITS.index(unit) for unit in POOL_ADA]
DIRECT_UNITS = [u for u in range(N_MIX) if u not in SPLIT_UNITS + POOL_UNITS]
N_DIRECT = len(DIRECT_UNITS)
BEFORE_MASKS = (5, 9)


def unit_of(name, i):
    return MIX_UNITS.index((name, i))


def build(nc, x, c, ada_w, ada_b, pre1_g, post1_g, pre2_g, post2_g, w_in, pool_w, pool_b, pool_scale,
          w_br_attn, w_br_pool, w_out, router_w, router_b, w_gu, b_gu, w_dn, b_dn, consts, out):
    bf16 = mybir.dt.bfloat16
    f32, i32, u32, f32r = mybir.dt.float32, mybir.dt.int32, mybir.dt.uint32, mybir.dt.float32r
    ALU = mybir.AluOpType
    ACT = mybir.ActivationFunctionType
    AX = mybir.AxisListType

    ctx = ExitStack()
    with ctx:
        def sb(name, shape, dt=f32):
            return ctx.enter_context(nc.sbuf_tensor(name, shape, dt))

        def sem(name):
            return ctx.enter_context(nc.semaphore(name))

        ring = sb("ring", [P, RING, SLOT_W])
        with nc.sbuf_tensor("act_hi", [P, DB, SEQ], f32r) as act_hi, \
                nc.sbuf_tensor("act_lo", [P, DB, SEQ], f32r) as act_lo, \
                nc.sbuf_tensor("w_hi", [P, PAIRS, PART_W], f32r) as w_hi, \
                nc.sbuf_tensor("w_lo", [P, PAIRS, PART_W], f32r) as w_lo:
            pass
        late = sb("late", [P, LATE, SLOT_W])
        const = sb("const", [P, CONST_W + SLOT_W - N_BANDS])
        rows = sb("rows", [N_ROWS, P])
        cols = sb("cols", [P, N_ROWS])
        x_sb = sb("x_sb", [P, TT, D])
        hT = sb("hT", [P, DB, SEQ])
        vu = sb("vu", [P, TT, D])
        merged = sb("merged", [P, TT, D])
        area = sb("area", [P, 4096])
        area2 = sb("area2", [P, 3 * 1536])
        area3 = sb("area3", [P, 6 * SEQ + PB * GROUP])
        spread = sb("spread", [P, D])
        bgu_sb = sb("bgu_sb", [3 * EXPERTS, 2 * F])
        bdn_sb = sb("bdn_sb", [EXPERTS, D])
        rw_sb = sb("rw_sb", [P, DB, EXPERTS])
        rb_sb = sb("rb_sb", [1, EXPERTS])
        modrow = sb("modrow", [P, BANK])
        mod = sb("mod", [P, 6 * DB])
        fac = sb("fac", [P, 4, DB])
        csig = sb("csig", [P, DB])
        cact = sb("cact", [P, DB, 32])
        stat = sb("stat", [P, 16])
        unread = sb("unread", [P, 8])
        top_v = sb("top_v", [P, TT, 8])
        top_i = sb("top_i", [P, TT, 8], u32)
        top_f = sb("top_f", [P, TT, TOP_K])
        top_e = sb("top_e", [P, TT, TOP_K])
        top_g = sb("top_g", [P, TT, TOP_K])
        logit = sb("logit", [P, TT, EXPERTS])
        logit0 = sb("logit0", [P, EXPERTS])
        mask = sb("mask", [P, TT, EXPERTS])
        gate = sb("gate", [P, TT, EXPERTS])
        rank = sb("rank", [P, TT, EXPERTS])
        nchunk = sb("nchunk", [EXPERTS, 4])
        base = sb("base", [1, 3 * EXPERTS + 1], i32)

        bands_end = CONSTS["band1"][1]

        def k(name):
            a, b = CONSTS[name]
            if a >= bands_end:
                a, b = a + SLOT_W - N_BANDS, b + SLOT_W - N_BANDS
            return const[:, a:b]

        def col(name, a=0, b=None):
            lo, hi = ROWS[name]
            return cols[:, lo + a:(lo + b if b is not None else hi)]

        ident, ones = k("ident"), k("ones")
        band0 = k("band0").rearrange("p (g t) -> p g t", t=SEQ)
        band1 = k("band1").rearrange("p (g t) -> p g t", t=P)
        slot = k("slot").rearrange("p (c s) -> p c s", s=P)
        gates = area[:, :].rearrange("p (t n) -> p t n", t=TT)
        qkT = area3[:, 0:4 * SEQ].rearrange("p (b t) -> p b t", t=SEQ)
        attnT = area3[:, 4 * SEQ:6 * SEQ].rearrange("p (b t) -> p b t", t=SEQ)
        poolw_sb = area3[:, 6 * SEQ:].rearrange("p (b d) -> p b d", d=GROUP)
        bands_at = CONSTS["tri_neg"][0]
        extra = [area2[:, 1024:3072], area3[:, 0:SLOT_W], const[:, bands_at:bands_at + SLOT_W],
                 vu.rearrange("p t n -> p (t n)")]
        xhat = merged
        sp0 = area2[:, 0:1024].rearrange("p (a b q) -> p a b q", a=2, b=2)
        sp1 = area2[:, 1024:1536].rearrange("p (a b q) -> p a b q", a=2, b=2)
        e0, e1 = area2[:, 1536:2560], area2[:, 2560:3072]
        a0 = area2[:, 3072:4096].rearrange("p (a b q) -> p a b q", a=2, b=2)
        a1 = area2[:, 4096:4608].rearrange("p (a b q) -> p a b q", a=2, b=2)
        ada_sum = [None, merged.rearrange("p t n -> p (t n)"), hT.rearrange("p b t -> p (b t)")]
        mixT = area2[:, 0:1536].rearrange("p (b t) -> p b t", t=SEQ)
        poolT = area2[:, 1536:3072].rearrange("p (b t) -> p b t", t=SEQ)
        prod = area2[:, 3072:3072 + 1024].rearrange("p (a n) -> p a n", a=2)
        diag = area2[:, 0:1024].rearrange("p (b n) -> p b n", n=P)
        junk = area2[:, 3072:4096]
        tail = area2[:, 1024:3072].rearrange("p (t n) -> p t n", t=TT)
        h2T = vu.rearrange("p t n -> p (t n)").rearrange("p (b t) -> p b t", t=SEQ)
        yspread, yacc = vu, merged
        hot = area[:, 1408:1664].rearrange("p (t r e) -> p t r e", t=TT, r=TOP_K)
        hotg = area[:, 1664:1920].rearrange("p (t r e) -> p t r e", t=TT, r=TOP_K)
        pick = area[:, 0:128].rearrange("p (t s) -> p t s", t=TT)
        pickg = area[:, 128:384].rearrange("p (t s) -> p t s", t=TT)
        xg = area[:, 384:896].rearrange("p (b s) -> p b s", s=CAP)
        xg_m = area[:, 896:1408].rearrange("p (b s) -> p b s", s=CAP)
        g_min, g_sig = area[:, 1408:1920], area[:, 1920:2432]
        u_clip, g_act, act_sb = area[:, 2432:2944], area[:, 2944:3456], area[:, 3456:3968]
        actT = area2[:, 3072:3584].rearrange("p (j s) -> p j s", s=P)
        ye = area2[:, 3584:4096]
        pickT = area2[:, 4096:4352]
        gateT = area2[0:EXPERTS, 4352:4608]
        esel = area[0:3 * EXPERTS, 3968:3968 + CAP // 2].bitcast(bf16)
        bgu_parts = hT.rearrange("p b t -> p (b t)")[0:3 * EXPERTS, 0:F].bitcast(bf16)

        ps = ctx.enter_context(nc.psum_tensor("ps", [P, 8, BANK], f32))
        xT_ps = ps[:, 0:4, :].rearrange("p k (b t) -> p (k b) t", t=SEQ)
        x2T_ps = ps[:, 0:4, :].rearrange("p (t k) (b n) -> p t (k b) n", t=TT, n=P)
        GATE, UP, GATHER, DOWN, TURN = range(5)

        const_in, rows_in, x_in, poolw_in, router_in, bias_in = map(
            sem, ("const_in", "rows_in", "x_in", "poolw_in", "router_in", "bias_in"))
        bgu_in, bgu_rounded, bgu_rest = sem("bgu_in"), sem("bgu_rounded"), sem("bgu_rest")
        unit_in = [sem(f"unit_in{i}") for i in range(SLOTS)]
        unit_used = sem("unit_used")
        ada_weighed = sem("ada_weighed")
        ada_added = sem("ada_added")
        hi_ready, lo_ready = sem("hi_ready"), sem("lo_ready")
        pair_used = sem("pair_used")
        act_hi_ready, act_lo_ready = sem("act_hi_ready"), sem("act_lo_ready")
        names = ("rows_turned", "cols_ready", "csig_ready", "cact_ready", "squares_ready", "var_ready",
                 "std_ready", "rstd_ready", "xhat_ready", "x_turned", "modrow_ready",
                 "modcol_done", "mod_ready", "h_low_ready", "q_done", "qk_ready", "in_done", "vu_ready",
                 "gates_ready", "z_done", "sp_part", "sp_ready", "sp_masked", "loga_done", "a_ready",
                 "a_masked", "o_done", "attnT_ready", "mix_done", "mixT_ready", "pool_done", "even_done",
                 "poolT_ready", "brA_done", "brA_ready", "brP_done", "brP_ready", "m_turned",
                 "diag_ready", "spread_done", "spread_ready", "x1_ready",
                 "x2_turned", "h2_ready", "h2b_ready", "logit_done", "logit_ready", "exp_ready",
                 "mask_ready", "gate_ready", "rank_done", "count_done", "nchunk_ready", "base_done",
                 "base_ready", "gateT_done", "gateT_ready", "bias_done", "dve_step",
                 "act_step", "out_done", "rank_ready", "y0_squared", "y1_spread", "shift_ready", "logit0_done",
                 "logit0_ready", "logits_here", "ada_done", "half_scattered", "y0_spread", "max_here", "ysum_ready")
        s = {n: sem(n) for n in names}
        names = ("pick_ready", "pickg_ready", "gathered", "xgm_ready", "xg_ready", "gu_done", "gmin_ready", "sig_ready",
                 "u_ready", "gact_ready", "act_ready", "turned", "actT_ready", "down_done", "ye_ready",
                 "pick_turned", "pickT_ready", "scattered", "acc_ready")
        m = {n: sem(n) for n in names}
        block = ctx.enter_context(nc.Block())

        def slot_of(u):
            return ring[:, u % RING, :]

        def part_of(p):
            u = SPLIT_UNITS[p // 2]
            return u, ring[:, u % RING, (p % 2) * PART_W:(p % 2 + 1) * PART_W]

        def slot_at(at):
            return ring[:, at, :] if at < RING else late[:, at - RING, :] if at < UNITS else extra[at - UNITS]

        def place(q):
            return ((N_MIX + q) % RING, (N_MIX + q) // RING) if q < RING else (q, 0)

        def expert_units(first, count, rnd, r):
            for j in range(first, first + count):
                at, in_mixer = place((UNITS * r + j) % SLOTS)
                yield at, 16 * (in_mixer + (UNITS * r + j) // SLOTS + 1) + 16 * TURNS * rnd

        def ge(engine, semaphore, value):
            if isinstance(value, int) and value <= 0:
                return
            engine.wait_ge(semaphore, value)

        def used(engine, name, i):
            u = unit_of(name, i)
            if u in SPLIT_UNITS:
                engine.wait_ge(pair_used, 2 * SPLIT_UNITS.index(u) + 2)
            else:
                engine.wait_ge(unit_used, DIRECT_UNITS.index(u) + 1)

        def added(engine, n):
            if n % DB == 0:
                engine.wait_ge(ada_weighed, n + 1)
            else:
                engine.wait_ge(ada_added, n - n // DB)

        def released(engine, u):
            if u in SPLIT_UNITS:
                engine.wait_ge(lo_ready, 2 * SPLIT_UNITS.index(u) + 2)
            elif u in POOL_UNITS:
                added(engine, POOL_UNITS.index(u))
            elif u >= 0:
                used(engine, *MIX_UNITS[u])

        def in_block_done(engine, n, t):
            if t == 0:
                engine.wait_ge(s["in_done"], n)
            else:
                used(engine, "w_in", 2 * n + 1)

        def branch_done(engine, semaphore, name, i, t, h):
            if (t, h) != (1, 1):
                engine.wait_ge(semaphore, 2 * t + h + 1)
            else:
                used(engine, name, i)

        @block.sync
        def _(sp):
            sp.dma_start(const[:, 0:CONST_FIRST], consts[:, 0:CONST_FIRST]).then_inc(const_in, 16)
            sp.dma_start(x_sb[:, :, :], x[0].rearrange("(t p) n -> p t n", p=P)).then_inc(x_in, 16)
            sp.wait_ge(rows_in, 16 * len(ROWS))
            ada_v = ada_w[0].rearrange("(k p) n -> p k n", p=P)
            win_v = w_in[0].rearrange("(k p) n -> p k n", p=P)
            for u, (name, i) in enumerate(MIX_UNITS):
                dst = slot_of(u)
                if name.startswith("ada"):
                    j = int(name[3])
                    src = ada_v[:, i, j * 2 * D:(j + 1) * 2 * D]
                elif name == "w_in":
                    n, half = i // 2, i % 2
                    dst = dst.rearrange("p (k n) -> p k n", n=BANK)
                    src = win_v[:, 4 * half:4 * half + 4, n * BANK:(n + 1) * BANK]
                else:
                    w = {"br_attn": w_br_attn, "br_pool": w_br_pool, "w_out": w_out}[name]
                    dst = dst.rearrange("p (k n) -> p k n", n=D)
                    src = w[0].rearrange("(k p) n -> p k n", p=P)[:, 2 * i:2 * i + 2, :]
                released(sp, u - RING)
                sp.dma_start(dst, src).then_inc(unit_in[u % RING], 16)

            def expert(rnd, r, used_before):
                e = ROUND * rnd + r
                for j in range(UNITS):
                    at = place((UNITS * r + j) % SLOTS)[0]
                    if j < GU_UNITS:
                        dst, src = slot_at(at), w_gu[0, e, j * P:(j + 1) * P, :]
                    else:
                        i = j - GU_UNITS
                        dst = slot_at(at).rearrange("p (k n) -> p k n", n=D)
                        src = w_dn[0, e, 2 * i * P:2 * (i + 1) * P, :].rearrange("(k p) n -> p k n", p=P)
                    used_before(UNITS * e + j)
                    sp.dma_start(dst, src).then_inc(unit_in[at], 16)

            def free_at_first(n):
                if n < RING:
                    released(sp, N_MIX + n - RING)
                elif n == RING:
                    sp.wait_ge(pair_used, PARTS)
                elif n == UNITS:
                    sp.wait_ge(act_lo_ready, 5)
                    used(sp, "br_attn", 0)
                elif n == SLOTS - 1:
                    sp.wait_ge(s["logit_done"], 1)
                elif n >= SLOTS:
                    free_again(n)

            def free_again(n):
                sp.wait_ge(unit_used, N_DIRECT + 1 - SLOTS + n)

            for r in range(ROUND):
                expert(0, r, free_at_first)
            with sp.Fori(1, EXPERTS // ROUND) as rnd:
                for r in range(ROUND):
                    expert(rnd, r, free_again)
            for t in range(TT):
                sp.wait_ge(s["out_done"], t + 1)
                sp.dma_start(out[0, t * P:(t + 1) * P, :], tail[:, t, :]).then_inc(x_in, 16)
            sp.wait_ge(x_in, 16 * (1 + TT))

        @block.tensor
        def _(pe):
            mm = nc.tensor.matmul

            def arrived(u):
                pe.wait_ge(unit_in[u % RING], 16 * (u // RING + 1))

            def parts_of(name, i):
                p0 = 2 * SPLIT_UNITS.index(unit_of(name, i))
                for p in (p0, p0 + 1):
                    pe.wait_ge(lo_ready, p + 1)
                    yield p % 2, w_hi[:, p % PAIRS, :], w_lo[:, p % PAIRS, :]

            def project_split(name, i, bank, n_k):
                for half, whi, wlo in parts_of(name, i):
                    kk = 2 * i + half
                    for t in range(TT):
                        at = slice(t * P, (t + 1) * P)
                        for h in range(2):
                            o, ws = ps[:, bank + 2 * t + h, :], slice(h * BANK, (h + 1) * BANK)
                            mm(o, act_hi[:, kk, at], whi[:, ws], start=(kk == 0), stop=False)
                            mm(o, act_hi[:, kk, at], wlo[:, ws], start=False, stop=False)
                            last = mm(o, act_lo[:, kk, at], whi[:, ws], start=False, stop=(kk == n_k - 1))
                            if kk == n_k - 1 and (t, h) != (1, 1) and name == "br_pool":
                                last.then_inc(s["brP_done"], 1)
                    last.then_inc(pair_used, 1)

            def ada_rows(j, bank):
                for kk in range(DB):
                    u = unit_of(f"ada{j}", kk)
                    arrived(u)
                    for q in range(4):
                        last = mm(ps[32 * q:32 * q + 32, bank, :], cact[:, kk, :],
                                  slot_of(u)[:, q * BANK:(q + 1) * BANK], start=(kk == 0), stop=(kk == DB - 1))
                    last.then_inc(unit_used, 1)

            def ada_summed(j, bank):
                added(pe, j * DB - 1)
                for q in range(4):
                    last = mm(ps[32 * q:32 * q + 32, bank, :], ones[:, 0:32],
                              ada_sum[j][:, q * BANK:(q + 1) * BANK], start=True, stop=True)
                last.then_inc(s["ada_done"], 1)

            def ada_cols(j, bank):
                pe.wait_ge(s["modrow_ready"], j + 1)
                view = ps[:, bank, 0:16].rearrange("p (q i) -> p i q", i=4)
                for i in range(4):
                    last = mm(view[:, i, :], modrow[:, i * P:(i + 1) * P], k("quad"), start=True, stop=True)
                last.then_inc(s["modcol_done"], 1)

            def keep_busy(products):
                for _ in range(products):
                    mm(ps[:, GATHER, :], ident, x_sb[:, 0, 0:BANK], start=True, stop=True)

            def spread_over(n, bank):
                pe.wait_ge(s["diag_ready"], n)
                for h in range(2):
                    last = mm(ps[:, bank + h, :], ones, diag[:, 4 * h:4 * h + 4, :], start=True, stop=True)
                last.then_inc(s["spread_done"], 1)

            pe.wait_ge(const_in, 16)
            pe.wait_ge(rows_in, 16 * len(ROWS))
            nc.tensor.transpose(ps[:, 5, 0:N_ROWS], rows[:, :], ident[0:N_ROWS, 0:N_ROWS])\
                .then_inc(s["rows_turned"], 1)
            for t in range(TT):
                pe.wait_ge(s["xhat_ready"], t + 1)
                for b in range(DB):
                    last = nc.tensor.transpose(xT_ps[:, b, t * P:(t + 1) * P], xhat[:, t, b * P:(b + 1) * P], ident)
            last.then_inc(s["x_turned"], 1)
            pe.wait_ge(s["cact_ready"], 1)
            ada_rows(0, 4)
            pe.wait_ge(s["cols_ready"], 1)
            ada_cols(0, 5)

            for half in range(2):
                for q, whi, wlo in parts_of("w_in", half):
                    pe.wait_ge(act_lo_ready, 2 * half + q + 1)
                    for k2 in range(2):
                        kk = 4 * half + 2 * q + k2
                        for fb in range(4):
                            o, ws = ps[:, 4 + fb, 0:SEQ], slice(k2 * BANK + fb * P, k2 * BANK + (fb + 1) * P)
                            mm(o, whi[:, ws], act_hi[:, kk, :], start=(kk == 0), stop=False)
                            mm(o, whi[:, ws], act_lo[:, kk, :], start=False, stop=False)
                            last = mm(o, wlo[:, ws], act_hi[:, kk, :], start=False, stop=(kk == DB - 1))
                            if kk == DB - 1 and fb == 1:
                                last.then_inc(s["q_done"], 1)
                    last.then_inc(pair_used, 1)

            def in_block(n):
                for half in range(2):
                    for q, whi, wlo in parts_of("w_in", 2 * n + half):
                        for t in range(TT):
                            at = slice(t * P, (t + 1) * P)
                            o = ps[:, 2 * ((n - 1) % 2) + t, :]
                            for k2 in range(2):
                                kk = 4 * half + 2 * q + k2
                                ws = slice(k2 * BANK, (k2 + 1) * BANK)
                                mm(o, act_hi[:, kk, at], whi[:, ws], start=(kk == 0), stop=False)
                                mm(o, act_hi[:, kk, at], wlo[:, ws], start=False, stop=False)
                                last = mm(o, act_lo[:, kk, at], whi[:, ws], start=False, stop=(kk == DB - 1))
                            if (half, q, t) == (1, 1, 0):
                                last.then_inc(s["in_done"], 1)
                        last.then_inc(pair_used, 1)

            in_block(1)
            in_block(2)

            def z_into(first):
                for head in range(HEADS):
                    par, b = head % 2, head // 2
                    q, kT = qkT[par * HD:par * HD + HD, b, :], qkT[par * HD:par * HD + HD, 2 + b, :]
                    mm(ps[:, 4 + par, b * SEQ:(b + 1) * SEQ], kT[:, 0:P], q, start=first, stop=True,
                       skip_group_check=not first)
                    last = mm(ps[:, 6 + par, b * P:(b + 1) * P], kT[:, P:SEQ], q[:, P:SEQ], start=first, stop=True,
                              skip_group_check=not first)
                return last

            pe.wait_ge(s["qk_ready"], 2)
            z_into(True).then_inc(s["z_done"], 1)
            pe.wait_ge(s["vu_ready"], 2)
            in_block(3)
            pe.wait_ge(s["vu_ready"], 4)
            in_block(4)
            pe.wait_ge(const_in, 48)
            pe.wait_ge(s["sp_masked"], 2)
            for par in range(2):
                mm(ps[:, 4 + par, :], k("tri_neg"), sp0[:, par], start=True, stop=True)
                mm(ps[:, 4 + par, :].rearrange("p (b q) -> p b q", b=2)[:, :, P:SEQ], k("ones_neg"), sp1[:, par],
                   start=False, stop=True, skip_group_check=True)
                mm(ps[:, 6 + par, 0:SEQ], k("tri_neg"), sp1[:, par], start=True, stop=True)
            z_into(False).then_inc(s["loga_done"], 1)
            pe.wait_ge(s["gates_ready"], 2)
            in_block(5)
            pe.wait_ge(s["a_masked"], 2)
            for head in range(HEADS):
                par, b = head % 2, head // 2
                o = ps[par * HD:par * HD + HD, 4, b * SEQ:(b + 1) * SEQ]
                mm(o, vu[:, 0, head * HD:(head + 1) * HD], a0[:, par, b, :], start=True, stop=True)
                last = mm(o[:, P:SEQ], vu[:, 1, head * HD:(head + 1) * HD], a1[:, par, b, :], start=False, stop=True,
                          skip_group_check=True)
            last.then_inc(s["o_done"], 1)
            for b in range(PB):
                for g in range(len(WINDOWS)):
                    lo, hi = max(b * P, g * GROUP), min((b + 1) * P, (g + 1) * GROUP)
                    if lo >= hi:
                        continue
                    o = ps[lo - b * P:hi - b * P, 5 + b // 2, (b % 2) * SEQ:(b % 2 + 1) * SEQ]
                    mm(o, vu[:, 0, ATTN_W + lo:ATTN_W + hi], band0[:, g, :], start=True, stop=True)
                    last = mm(o[:, P:SEQ], vu[:, 1, ATTN_W + lo:ATTN_W + hi], band1[:, g, :], start=False, stop=True,
                              skip_group_check=True)
            last.then_inc(s["mix_done"], 1)
            pe.wait_ge(s["gates_ready"], 4)
            in_block(6)
            pe.wait_ge(poolw_in, 16)
            pe.wait_ge(s["mixT_ready"], 1)

            def parts(g):
                found = []
                for b in range(PB):
                    lo, hi = max(b * P, g * GROUP), min((b + 1) * P, (g + 1) * GROUP)
                    if lo < hi:
                        found.append((b, lo - b * P, hi - b * P))
                return sorted(found, key=lambda f: f[2] - f[1])

            for g in (0, 2, 1, 3):
                if g == 1:
                    pe.wait_ge(s["even_done"], 1)
                for ob, olo, ohi in parts(g):
                    d0 = ob * P + olo - g * GROUP
                    ins = parts(g)
                    for n, (ib, ilo, ihi) in enumerate(ins):
                        last = mm(ps[olo:ohi, 5 + ob // 2, (ob % 2) * SEQ:(ob % 2 + 1) * SEQ],
                                  poolw_sb[ilo:ihi, ib, d0:d0 + ohi - olo], mixT[ilo:ihi, ib, :],
                                  start=(n == 0), stop=(n == len(ins) - 1))
                if g == 2:
                    last.then_inc(s["even_done"], 1)
            last.then_inc(s["pool_done"], 1)
            pe.wait_ge(s["attnT_ready"], 1)
            ada_summed(1, 4)
            pe.wait_ge(s["gates_ready"], 8)
            arrived(unit_of("br_attn", 0))
            w = slot_of(unit_of("br_attn", 0)).rearrange("p (k n) -> p k n", n=D)
            for t in range(TT):
                for h in range(2):
                    for b in range(2):
                        last = mm(ps[:, 2 * t + h, :], attnT[:, b, t * P:(t + 1) * P],
                                  w[:, b, h * BANK:(h + 1) * BANK], start=(b == 0), stop=(b == 1))
                    if (t, h) != (1, 1):
                        last.then_inc(s["brA_done"], 1)
            last.then_inc(unit_used, 1)
            pe.wait_ge(act_lo_ready, 5)
            for i in range(3):
                project_split("br_pool", i, 4, PB)
            pe.wait_ge(s["brA_ready"], 4)
            ada_cols(1, 0)
            ada_summed(2, 1)
            mT_ps = ps[:, 4:8, :].rearrange("p k (b t) -> p (k b) t", t=SEQ)
            for t in range(TT):
                pe.wait_ge(s["brP_ready"], 4)
                for b in range(DB):
                    last = nc.tensor.transpose(mT_ps[:, b, t * P:(t + 1) * P], merged[:, t, b * P:(b + 1) * P], ident)
            last.then_inc(s["m_turned"], 1)
            pe.wait_ge(s["mod_ready"], 2)
            pe.wait_ge(s["modrow_ready"], 3)
            pe.wait_ge(act_lo_ready, 6)
            project_split("w_out", 0, 0, DB)
            pe.wait_ge(act_lo_ready, 9)
            project_split("w_out", 1, 0, DB)
            spread_over(1, 6)
            ada_cols(2, 5)
            project_split("w_out", 2, 0, DB)
            pe.wait_ge(s["shift_ready"], 1)
            pe.wait_ge(router_in, 32)
            for kk in range(DB):
                mm(ps[:, 4, 0:EXPERTS], diag[:, kk, :], rw_sb[:, kk, :], start=(kk == 0), stop=False)
            mm(ps[:, 4, 0:EXPERTS], ones[0:1, :], rb_sb[0:1, :], start=False, stop=True)\
                .then_inc(s["logit0_done"], 1)
            project_split("w_out", 3, 0, DB)
            pe.wait_ge(s["spread_ready"], 1)
            spread_over(2, 6)
            for t in range(TT):
                pe.wait_ge(s["x1_ready"], t + 1)
                for b in range(DB):
                    last = nc.tensor.transpose(x2T_ps[:, t, b, :], x_sb[:, t, b * P:(b + 1) * P], ident)
                last.then_inc(s["x2_turned"], 1)
            for t in range(TT):
                pe.wait_ge(s["h2_ready"] if t == 0 else s["h2b_ready"], 1)
                o = ps[:, 5, t * EXPERTS:(t + 1) * EXPERTS]
                for kk in range(DB):
                    last = mm(o, h2T[:, kk, t * P:(t + 1) * P], rw_sb[:, kk, :], start=(kk == 0), stop=(kk == DB - 1))
            last.then_inc(s["logit_done"], 1)
            keep_busy(2)
            pe.wait_ge(s["mask_ready"], 1)
            for t in range(TT):
                last = mm(ps[0:EXPERTS, 4, 0:1], mask[:, t, :], ones[:, 0:1], start=(t == 0), stop=(t == 1))
            last.then_inc(s["count_done"], 1)
            mm(ps[:, 3, 0:EXPERTS], k("before"), mask[:, 0, :], start=True, stop=True)
            mm(ps[:, 3, EXPERTS:2 * EXPERTS], k("before"), mask[:, 1, :], start=True, stop=False)
            mm(ps[:, 3, EXPERTS:2 * EXPERTS], ones, mask[:, 0, :], start=False, stop=True)\
                .then_inc(s["rank_done"], 1)
            pe.wait_ge(s["nchunk_ready"], 1)
            mm(ps[0:1, 5, 0:EXPERTS + 1], nchunk[:, 0:1], k("before_e")[0:EXPERTS, :], start=True, stop=True)
            mm(ps[0:1, 5, EXPERTS + 1:2 * EXPERTS + 1], nchunk[:, 0:1], ident[0:EXPERTS, 0:EXPERTS],
               start=True, stop=True).then_inc(s["base_done"], 1)
            keep_busy(1)

            def output_bias():
                pe.wait_ge(s["spread_ready"], 2)
                pe.wait_ge(s["gate_ready"], 1)
                for t in range(TT):
                    last = nc.tensor.transpose(ps[0:EXPERTS, 4, t * P:(t + 1) * P], gate[:, t, :], ident)
                last.then_inc(s["gateT_done"], 1)
                pe.wait_ge(s["gateT_ready"], 1)
                pe.wait_ge(bias_in, 16)
                for t in range(TT):
                    for h in range(2):
                        last = mm(ps[:, TURN + 2 * t + h, :], gateT[:, t * P:(t + 1) * P],
                                  bdn_sb[:, h * BANK:(h + 1) * BANK], start=True, stop=True)
                last.then_inc(s["bias_done"], 1)

            def gather(g):
                pe.wait_ge(m["pick_ready"], g + 1)
                for b in range(DB):
                    for t in range(TT):
                        last = mm(ps[:, GATHER, b * CAP:(b + 1) * CAP], x_sb[:, t, b * P:(b + 1) * P],
                                  pick[:, t, :], start=(t == 0), stop=(t == TT - 1))
                last.then_inc(m["gathered"], 1)

            def turn_pick(g):
                pe.wait_ge(m["pickg_ready"], g + 1)
                for t in range(TT):
                    last = nc.tensor.transpose(ps[:, DOWN, t * P:(t + 1) * P], pickg[:, t, :], ident)
                last.then_inc(m["pick_turned"], 1)

            def scatter(g, end=False):
                ge(pe, m["ye_ready"], g)
                ge(pe, m["pickT_ready"], g)
                for t in range(TT):
                    for h in range(2):
                        last = mm(ps[:, TURN + 2 * t + h, :], pickT[CAP * h:CAP * h + CAP, t * P:(t + 1) * P],
                                  ye[CAP * h:CAP * h + CAP, :], start=True, stop=True)
                    if end and t == 0:
                        last.then_inc(s["half_scattered"], 1)
                last.then_inc(m["scattered"], 1)

            outs = [(ps[CAP * h:CAP * h + CAP, bank, :], (2 * bank + h) * BANK)
                    for bank in (GATE, UP) for h in range(2)]

            def biases():
                for o, c0 in outs:
                    mm(o, esel, bgu_parts[:, c0:c0 + BANK], start=True, stop=False)

            def down(g, rnd, r, release, end=False):
                if end:
                    keep_busy(3)
                pe.wait_ge(m["act_ready"], g)
                pe.wait_ge(m["acc_ready"], g)
                for j in range(4):
                    last = nc.tensor.transpose(ps[:, TURN, j * P:(j + 1) * P], act_sb[:, j * P:(j + 1) * P], ident)
                    if release and j == 0:
                        last.then_inc(unit_used, 1)
                last.then_inc(m["turned"], 1)
                if not end:
                    biases()
                pe.wait_ge(m["actT_ready"], g)
                arrivals = list(expert_units(GU_UNITS, DN_UNITS, rnd, r))
                for fb in range(DB):
                    at, count = arrivals[fb // 2]
                    if fb % 2 == 0:
                        pe.wait_ge(unit_in[at], count)
                    w = slot_at(at).rearrange("p (k n) -> p k n", n=D)
                    lhs = actT[:, fb % 4, (fb // 4) * CAP:(fb // 4 + 1) * CAP]
                    for h in range(2):
                        last = mm(ps[CAP * h:CAP * h + CAP, DOWN, :], lhs, w[:, fb % 2, h * BANK:(h + 1) * BANK],
                                  start=(fb == 0), stop=(fb == DB - 1))
                        if release and fb and fb % 2 == 0 and h == 0:
                            last.then_inc(unit_used, 1)
                last.then_inc(m["down_done"], 1)

            def gate_up(g, rnd, r, release, release_before, first=False):
                if first:
                    biases()
                pe.wait_ge(m["xg_ready"], g + 1)
                for kk, (at, count) in enumerate(expert_units(0, GU_UNITS, rnd, r)):
                    pe.wait_ge(unit_in[at], count)
                    for n, (o, c0) in enumerate(outs):
                        last = mm(o, xg[:, kk, :], slot_at(at)[:, c0:c0 + BANK], start=False, stop=(kk == DB - 1))
                        if release_before and kk == 0 and n == 0:
                            last.then_inc(unit_used, 1)
                        if release and kk and n == 0:
                            last.then_inc(unit_used, 1)
                    if kk == 1:
                        if not first:
                            scatter(g)
                        turn_pick(g)
                last.then_inc(m["gu_done"], 1)

            def chunk(g, of, of_before, last, last_before):
                gather(g)
                down(g, *of_before, last_before)
                gate_up(g, *of, last, last_before)

            def first_chunk(last):
                gather(0)
                pe.wait_ge(bgu_rounded, 4)
                gate_up(0, 0, 0, last, False, first=True)
                output_bias()

            def expert(rnd, r):
                e, of, of_before = ROUND * rnd + r, (rnd, r), (rnd, r - 1) if r else (rnd - 1, ROUND - 1)

                def start(b0, last):
                    if isinstance(e, int) and e == 0:
                        first_chunk(last)
                    else:
                        chunk(b0, of, of_before, last, True)

                n = pe.value_load(base[0:1, bass.ds(e + EXPERTS + 1, 1)], min_val=1, max_val=CHUNKS)
                b0 = pe.value_load(base[0:1, bass.ds(e, 1)], min_val=0, max_val=MAX_CHUNKS)
                with pe.If(n > 1):
                    start(b0, False)
                    with pe.If(n > 2):
                        with pe.Fori(1, n - 1) as c:
                            chunk(b0 + c, of, of, False, False)
                    final = pe.value_load(base[0:1, bass.ds(e + 2 * EXPERTS + 1, 1)], min_val=1,
                                          max_val=MAX_CHUNKS)
                    chunk(final, of, of, True, False)
                with pe.Else():
                    start(b0, True)

            pe.wait_ge(s["base_ready"], 2)
            for r in range(ROUND):
                expert(0, r)
            with pe.Fori(1, EXPERTS // ROUND) as rnd:
                for r in range(ROUND):
                    expert(rnd, r)
            n = pe.value_load(base[0:1, EXPERTS:EXPERTS + 1], min_val=EXPERTS, max_val=MAX_CHUNKS)
            down(n, EXPERTS // ROUND - 1, ROUND - 1, False, end=True)
            scatter(n, end=True)

        @block.scalar
        def _(act):
            A = nc.scalar.activation
            steps = [0]

            def link(ins):
                steps[0] += 1
                ins.then_inc(s["act_step"], 1)
                act.wait_ge(s["act_step"], steps[0])

            for name, src in (("ada_b", ada_b), ("pre1_g", pre1_g), ("post1_g", post1_g), ("pre2_g", pre2_g),
                              ("post2_g", post2_g), ("c", c)):
                lo, hi = ROWS[name]
                act.dma_start(rows[lo:hi, :], src[0].rearrange("(r p) -> r p", p=P)).then_inc(rows_in, 16)
            for name, src in (("pool_b", pool_b), ("pool_scale", pool_scale)):
                lo, hi = ROWS[name]
                act.dma_start(rows[lo:hi, :], src[0].rearrange("g n -> (g n)").rearrange("(r p) -> r p", p=P))\
                    .then_inc(rows_in, 16)

            tables = [-1]

            def load_table(func):
                tables[0] += 1
                A(unread[:, tables[0]:tables[0] + 1], ident[:, 0:1], func)

            def early_loads():
                act.dma_start(const[:, CONST_FIRST:bands_end], consts[:, CONST_FIRST:bands_end]).then_inc(const_in, 16)
                act.dma_start(const[:, bands_end + SLOT_W - N_BANDS:], consts[:, bands_end:]).then_inc(const_in, 16)
                act.dma_start(poolw_sb, pool_w[0].rearrange("g n d -> (g n) d")
                              .rearrange("(b p) d -> p b d", p=P)).then_inc(poolw_in, 16)

            def late_loads():
                act.dma_start(rw_sb[:, :, :], router_w[0].rearrange("(k p) e -> p k e", p=P)).then_inc(router_in, 16)
                act.dma_start(rb_sb[:, :], router_b).then_inc(router_in, 16)
                for part in range(3):
                    act.dma_start(bgu_sb[EXPERTS * part:EXPERTS * (part + 1), :], b_gu[0]).then_inc(bgu_in, 16)
                act.dma_start(bdn_sb[:, :], b_dn[0]).then_inc(bias_in, 16)

            def square_sums(src, at, done):
                for t in range(TT):
                    link(A(junk, src[:, t, :], ACT.Square, accum_out=stat[:, at + t:at + t + 1]))
                nc.scalar.activation(stat[:, 12:13], stat[:, at:at + 1], ACT.Copy).then_inc(s[done], 1)

            def std(n, at):
                act.wait_ge(s["var_ready"], n)
                A(stat[:, at:at + TT], stat[:, at:at + TT], ACT.Sqrt).then_inc(s["std_ready"], 1)

            def normed(n, at, src, dst, done):
                act.wait_ge(s["rstd_ready"], n)
                for t in range(TT):
                    A(dst[:, t, :], src[:, t, :], ACT.Copy, scale=stat[:, at + t:at + t + 1]).then_inc(s[done], 1)

            act.wait_ge(const_in, 16)
            load_table(ACT.Sqrt)
            act.wait_ge(x_in, 16)
            square_sums(x_sb, 0, "squares_ready")
            std(1, 0)
            normed(1, 0, x_sb, xhat, "xhat_ready")
            act.wait_ge(s["cols_ready"], 1)
            A(csig[:, :], col("c"), ACT.Sigmoid).then_inc(s["csig_ready"], 1)

            def split_hi(*which, weighing=True):
                for p in which:
                    u, raw = part_of(p)
                    if p % 2 == 0:
                        act.wait_ge(unit_in[u % RING], 16 * (u // RING + 1))
                    ge(act, pair_used, p - PAIRS + 1)
                    A(w_hi[:, p % PAIRS, :], raw, ACT.Copy).then_inc(hi_ready, 1)
                    if p % 2 and weighing:
                        weigh(u + 1)

            def weigh(u):
                while u < N_MIX and u not in SPLIT_UNITS:
                    if u in POOL_UNITS:
                        n = POOL_UNITS.index(u)
                        act.wait_ge(unit_in[u % RING], 16 * (u // RING + 1))
                        if n == DB:
                            act.wait_ge(act_lo_ready, 4)
                        A(ada_sum[1 + n // DB] if n % DB == 0 else slot_of(u), slot_of(u), ACT.Copy,
                          scale=cact[:, n % DB, 0:1]).then_inc(ada_weighed, 1)
                    u += 1

            act.wait_ge(s["cact_ready"], 1)
            split_hi(0)
            act.wait_ge(s["x_turned"], 1)
            act.wait_ge(s["mod_ready"], 1)
            for c2 in range(4):
                if c2 < 2:
                    act.wait_ge(s["h_low_ready"], c2 + 1)
                elif c2 == 2:
                    for b in range(4, DB):
                        last = A(hT[:, b, :], xT_ps[:, b, :], ACT.Identity, scale=fac[:, 0, b:b + 1],
                                 bias=mod[:, b:b + 1])
                    link(last)
                A(act_hi[:, 2 * c2:2 * c2 + 2, :], hT[:, 2 * c2:2 * c2 + 2, :], ACT.Copy).then_inc(act_hi_ready, 1)
                if c2 < 2:
                    split_hi(c2 + 1)
            split_hi(3, 4, 5)
            for n, scale in ((0, HD ** -0.5), (1, 1.0)):
                if n == 0:
                    act.wait_ge(s["q_done"], 1)
                else:
                    used(act, "w_in", 1)
                A(qkT[:, 2 * n:2 * n + 2, :], ps[:, 4 + 2 * n:6 + 2 * n, 0:SEQ], ACT.Copy, scale=scale)\
                    .then_inc(s["qk_ready"], 1)
            split_hi(*range(6, 14))
            early_loads()
            z0, z1 = ps[:, 4:6, :], ps[:, 6:8, 0:SEQ]
            e0v, e1v = e0.rearrange("p (a n) -> p a n", a=2), e1.rearrange("p (a n) -> p a n", a=2)
            act.wait_ge(s["z_done"], 1)
            A(e0v, z0, ACT.Abs).then_inc(s["act_step"], 1)
            A(e1v, z1, ACT.Abs).then_inc(s["act_step"], 1)
            steps[0] += 2
            act.wait_ge(s["act_step"], steps[0])
            for p, func, scale, bias in ((14, ACT.Exp, -1.0, 0.0), (15, ACT.Ln, 1.0, 1.0)):
                split_hi(p, weighing=False)
                link(A(area2[:, 1536:3072], area2[:, 1536:3072], func, scale=scale, bias=bias))
            A(stat[:, 13:14], stat[:, 0:1], ACT.Copy).then_inc(s["sp_part"], 1)

            def gate_block(n):
                for t in range(TT):
                    in_block_done(act, n, t)
                    A(gates[:, t, (n - 3) * BANK:(n - 2) * BANK], ps[:, 2 * ((n - 1) % 2) + t, :], ACT.Sigmoid)\
                        .then_inc(s["gates_ready"], 1)

            split_hi(16)
            weigh(part_of(15)[0] + 1)
            split_hi(17)
            gate_block(3)
            split_hi(18, 19, 20, 21)
            gate_block(4)
            split_hi(22)
            act.wait_ge(s["loga_done"], 1)
            A(a0, z0.rearrange("p a (b q) -> p a b q", b=2), ACT.Exp).then_inc(s["a_ready"], 1)
            A(a1, z1.rearrange("p a (b q) -> p a b q", b=2), ACT.Exp).then_inc(s["a_ready"], 1)
            split_hi(23, 24, 25)
            gate_block(5)
            split_hi(26)
            act.wait_ge(s["o_done"], 1)
            A(attnT, ps[:, 4, :].rearrange("p (b t) -> p b t", t=SEQ), ACT.Copy)\
                .then_inc(s["attnT_ready"], 1)
            split_hi(27)
            late_loads()
            split_hi(28, 29)
            gate_block(6)
            split_hi(30)
            act.wait_ge(s["poolT_ready"], 1)
            A(act_hi[:, 0:PB, :], poolT, ACT.Copy).then_inc(act_hi_ready, 1)
            split_hi(*range(31, 37))
            act.wait_ge(s["ada_done"], 2)
            A(modrow[:, :], ps[:, 1, :], ACT.Copy).then_inc(s["modrow_ready"], 1)
            act.wait_ge(s["m_turned"], 1)
            for n in range(4):
                A(act_hi[:, 2 * n:2 * n + 2, :], ps[:, 4 + n, :].rearrange("p (b t) -> p b t", t=SEQ), ACT.Copy)\
                    .then_inc(act_hi_ready, 1)
            def round_bias(first, rests):
                ge(act, bgu_rest, rests)
                at = slice(EXPERTS * first, 3 * EXPERTS if first != 1 else 2 * EXPERTS)
                A(bgu_parts[at], bgu_sb[at, :], ACT.Copy).then_inc(bgu_rounded, 1)

            split_hi(37)
            act.wait_ge(bgu_in, 48)
            round_bias(0, 0)
            split_hi(*range(38, PARTS))
            round_bias(1, 1)
            round_bias(2, 2)
            load_table(ACT.Sqrt)
            y_ps = ps[:, 0:4, :].rearrange("p (t h) n -> p t (h n)", t=TT)
            used(act, "w_out", 3)
            A(junk, y_ps[:, 0, :], ACT.Square, accum_out=stat[:, 2:3]).then_inc(s["y0_squared"], 1)
            act.wait_ge(s["y1_spread"], 1)
            act.wait_ge(s["y0_squared"], 1)
            link(A(junk, y_ps[:, 1, :], ACT.Square, accum_out=stat[:, 3:4]))
            A(stat[:, 12:13], stat[:, 2:3], ACT.Copy).then_inc(s["squares_ready"], 1)
            std(2, 2)
            for t in range(TT):
                act.wait_ge(s["x1_ready"], t + 1)
                link(A(junk, x_sb[:, t, :], ACT.Square, accum_out=stat[:, 4 + t:5 + t]))
            A(stat[:, 12:13], stat[:, 4:5], ACT.Copy).then_inc(s["squares_ready"], 1)
            std(3, 4)
            act.wait_ge(s["x2_turned"], 2)
            A(h2T[:, :, P:], x2T_ps[:, 1], ACT.Copy).then_inc(s["h2b_ready"], 1)
            load_table(ACT.Exp)
            act.wait_ge(s["spread_done"], 2)
            A(spread[:, :].rearrange("p (h n) -> p h n", h=2), ps[:, 6:8, :], ACT.Copy)\
                .then_inc(s["spread_ready"], 1)
            act.wait_ge(s["logit_ready"], 1)
            A(top_e[:, :, :], top_f[:, :, :], ACT.Exp).then_inc(s["exp_ready"], 1)
            round_bias(2, 3)
            load_table(ACT.Sigmoid)

            def back(g, end=False):
                act.wait_ge(m["gmin_ready"], g)
                A(g_sig, g_min, ACT.Sigmoid, scale=ALPHA).then_inc(m["sig_ready"], 1)
                act.wait_ge(m["turned"], g)
                A(actT, ps[:, TURN, :].rearrange("p (j s) -> p j s", s=P), ACT.Copy).then_inc(m["actT_ready"], 1)
                if end:
                    load_table(ACT.Sqrt)
                act.wait_ge(m["down_done"], g)
                A(ye, ps[:, DOWN, :], ACT.Copy).then_inc(m["ye_ready"], 1)

            def front(g):
                act.wait_ge(m["pick_turned"], g + 1)
                A(pickT, ps[:, DOWN, 0:2 * P], ACT.Copy).then_inc(m["pickT_ready"], 1)

            act.wait_ge(s["base_ready"], 2)

            def more_chunks(e):
                b0 = act.value_load(base[0:1, bass.ds(e, 1)], min_val=0, max_val=MAX_CHUNKS)
                n = act.value_load(base[0:1, bass.ds(e + EXPERTS + 1, 1)], min_val=1, max_val=CHUNKS)
                with act.If(n > 1):
                    with act.Fori(1, n) as c:
                        back(b0 + c)
                        front(b0 + c)

            front(0)
            act.wait_ge(s["gateT_done"], 1)
            A(gateT[:, :], ps[0:EXPERTS, 4, 0:SEQ], ACT.Copy).then_inc(s["gateT_ready"], 1)
            act.wait_ge(s["bias_done"], 1)
            A(yacc[:, :, :], ps[:, TURN:8, :].rearrange("p (t h) n -> p t (h n)", t=TT), ACT.Copy)\
                .then_inc(m["acc_ready"], 1)
            more_chunks(0)
            with act.Fori(1, EXPERTS) as e:
                b0 = act.value_load(base[0:1, bass.ds(e, 1)], min_val=1, max_val=MAX_CHUNKS)
                back(b0)
                front(b0)
                more_chunks(e)
            n = act.value_load(base[0:1, EXPERTS:EXPERTS + 1], min_val=EXPERTS, max_val=MAX_CHUNKS)
            back(n, end=True)
            for t in range(TT):
                act.wait_ge(s["ysum_ready"], t + 1)
                link(A(area[:, 384:384 + D], yacc[:, t, :], ACT.Square, accum_out=stat[:, 6 + t:7 + t]))
                A(stat[:, 12:13], stat[:, 6 + t:7 + t], ACT.Copy).then_inc(s["squares_ready"], 1)
                act.wait_ge(s["var_ready"], 4 + t)
                A(stat[:, 6 + t:7 + t], stat[:, 6 + t:7 + t], ACT.Sqrt).then_inc(s["std_ready"], 1)

        @block.gpsimd
        def _(pool):
            def causal(tile, width, done):
                nc.gpsimd.affine_select(out=tile, in_=tile, compare_op=ALU.is_gt, fill=0.0, base=0,
                                        pattern=[[0, 2], [0, 2], [1, width]], channel_multiplier=-1).then_inc(done, 1)

            def add(units):
                for n in units:
                    if n % DB == 0:
                        continue
                    total = ada_sum[1 + n // DB]
                    pool.wait_ge(ada_weighed, n + 1)
                    if n % DB > 1:
                        added(pool, n - 1)
                    nc.gpsimd.tensor_tensor(total, total, slot_of(POOL_UNITS[n]), ALU.add).then_inc(ada_added, 1)

            add(range(0, BEFORE_MASKS[0]))
            pool.wait_ge(s["sp_ready"], 2)
            causal(sp0, SEQ, s["sp_masked"])
            causal(sp1, P, s["sp_masked"])
            add(range(*BEFORE_MASKS))
            pool.wait_ge(s["a_ready"], 2)
            causal(a0, SEQ, s["a_masked"])
            causal(a1, P, s["a_masked"])
            add(range(BEFORE_MASKS[1], 2 * DB))

            def bias_rest(copy, rounded):
                pool.wait_ge(bgu_rounded, rounded)
                at = slice(EXPERTS * copy, EXPERTS * (copy + 1))
                nc.gpsimd.tensor_tensor(bgu_sb[at, :], bgu_sb[at, :], bgu_parts[at], ALU.subtract)\
                    .then_inc(bgu_rest, 1)

            bias_rest(1, 1)
            bias_rest(2, 1)
            bias_rest(2, 3)
            pool.wait_ge(s["spread_ready"], 2)
            pool.wait_ge(s["ysum_ready"], 1)
            nc.gpsimd.tensor_tensor(yspread[:, 0, :], yacc[:, 0, :], spread[:, :], ALU.mult)\
                .then_inc(s["y0_spread"], 1)

        @block.vector
        def _(dve):
            V = nc.vector
            steps = [0]

            def link(ins):
                steps[0] += 1
                ins.then_inc(s["dve_step"], 1)
                dve.wait_ge(s["dve_step"], steps[0])

            def variance(n, at, width=TT):
                dve.wait_ge(s["squares_ready"], n)
                V.tensor_scalar(stat[:, at:at + width], stat[:, at:at + width], 1.0 / D, EPS, ALU.mult, ALU.add)\
                    .then_inc(s["var_ready"], 1)

            def rstd(n, at, done=True, width=TT):
                dve.wait_ge(s["std_ready"], n)
                ins = V.reciprocal(stat[:, at:at + width], stat[:, at:at + width])
                if done:
                    ins.then_inc(s["rstd_ready"], 1)
                else:
                    link(ins)

            def over(ap, n):
                return ap.unsqueeze(2).broadcast_to([ap.shape[0], ap.shape[1], n])

            dve.wait_ge(s["rows_turned"], 1)
            V.tensor_copy(cols[:, :], ps[:, 5, 0:N_ROWS]).then_inc(s["cols_ready"], 1)
            variance(1, 0)
            rstd(1, 0)
            dve.wait_ge(s["csig_ready"], 1)
            dve.wait_ge(s["cols_ready"], 1)
            V.tensor_tensor(cact[:, :, :], over(col("c"), 32), over(csig[:, :], 32), ALU.mult)\
                .then_inc(s["cact_ready"], 1)

            def mod_rows(j, bank):
                if j == 0:
                    used(dve, "ada0", DB - 1)
                else:
                    dve.wait_ge(s["ada_done"], 1)
                V.tensor_copy(modrow[:, :], ps[:, bank, :]).then_inc(s["modrow_ready"], 1)

            def mod_cols(j, bank):
                dve.wait_ge(s["modcol_done"], j + 1)
                link(V.tensor_tensor(mod[:, 16 * j:16 * j + 16], ps[:, bank, 0:16], col("ada_b", 16 * j, 16 * j + 16),
                                     ALU.add))

            def factor(f, at, gain, plus):
                return V.scalar_tensor_tensor(out=fac[:, f, :], in0=mod[:, at:at + DB], scalar=plus, in1=col(gain),
                                              op0=ALU.add, op1=ALU.mult)

            def split_lo(*which):
                for p in which:
                    dve.wait_ge(hi_ready, p + 1)
                    V.tensor_tensor(w_lo[:, p % PAIRS, :], part_of(p)[1], w_hi[:, p % PAIRS, :].bitcast(f32),
                                    ALU.subtract).then_inc(lo_ready, 1)

            def act_lo_from(n, src, a, b):
                dve.wait_ge(act_hi_ready, n)
                V.tensor_tensor(act_lo[:, a:b, :], src, act_hi[:, a:b, :].bitcast(f32), ALU.subtract)\
                    .then_inc(act_lo_ready, 1)

            mod_rows(0, 4)
            mod_cols(0, 5)
            link(factor(0, DB, "pre1_g", 1.0))
            V.tensor_copy(stat[:, 14:15], stat[:, 0:1]).then_inc(s["mod_ready"], 1)
            dve.wait_ge(s["x_turned"], 1)
            for b in range(4):
                last = V.tensor_scalar(hT[:, b, :], xT_ps[:, b, :], fac[:, 0, b:b + 1], mod[:, b:b + 1],
                                       ALU.mult, ALU.add)
                if b % 2:
                    last.then_inc(s["h_low_ready"], 1)
            for c2 in range(4):
                if c2 < 2:
                    dve.wait_ge(s["h_low_ready"], c2 + 1)
                act_lo_from(c2 + 1, hT[:, 2 * c2:2 * c2 + 2, :], 2 * c2, 2 * c2 + 2)
                split_lo(c2)
            split_lo(*range(4, 10))
            for n in (1, 2):
                for t in range(TT):
                    in_block_done(dve, n, t)
                    V.tensor_copy(vu[:, t, (n - 1) * BANK:n * BANK], ps[:, 2 * (n - 1) + t, :])\
                        .then_inc(s["vu_ready"], 1)
                split_lo(*(range(10, 14) if n == 1 else range(14, 16)))
            z0, z1 = ps[:, 4:6, :], ps[:, 6:8, 0:SEQ]
            dve.wait_ge(s["sp_part"], 1)
            V.scalar_tensor_tensor(out=area2[:, 0:1024].rearrange("p (a n) -> p a n", a=2), in0=z0, scalar=0.0,
                                   in1=e0.rearrange("p (a n) -> p a n", a=2), op0=ALU.max, op1=ALU.add)\
                .then_inc(s["sp_ready"], 1)
            V.scalar_tensor_tensor(out=area2[:, 1024:1536].rearrange("p (a n) -> p a n", a=2), in0=z1, scalar=0.0,
                                   in1=e1.rearrange("p (a n) -> p a n", a=2), op0=ALU.max, op1=ALU.add)\
                .then_inc(s["sp_ready"], 1)
            split_lo(*range(16, 27))
            dve.wait_ge(s["mix_done"], 1)
            V.tensor_copy(mixT, ps[:, 5:8, :].rearrange("p k (b t) -> p (k b) t", t=SEQ)).then_inc(s["mixT_ready"], 1)
            split_lo(*range(27, 31))
            dve.wait_ge(s["pool_done"], 1)
            for b in range(PB):
                last = V.tensor_scalar(poolT[:, b, :], ps[:, 5 + b // 2, (b % 2) * SEQ:(b % 2 + 1) * SEQ],
                                       col("pool_b", b, b + 1), col("pool_scale", b, b + 1), ALU.add, ALU.mult)
            last.then_inc(s["poolT_ready"], 1)
            dve.wait_ge(s["poolT_ready"], 1)
            mod_rows(1, 4)
            act_lo_from(5, poolT, 0, PB)
            split_lo(31)
            for t in range(TT):
                for h in range(2):
                    branch_done(dve, s["brA_done"], "br_attn", 0, t, h)
                    V.tensor_tensor(merged[:, t, h * BANK:(h + 1) * BANK], ps[:, 2 * t + h, :],
                                    gates[:, t, h * BANK:(h + 1) * BANK], ALU.mult).then_inc(s["brA_ready"], 1)
            split_lo(32, 33)
            for t in range(TT):
                for h in range(2):
                    branch_done(dve, s["brP_done"], "br_pool", 2, t, h)
                    link(V.tensor_tensor(prod[:, h, :], ps[:, 4 + 2 * t + h, :],
                                         gates[:, t, D + h * BANK:D + (h + 1) * BANK], ALU.mult))
                    half = merged[:, t, h * BANK:(h + 1) * BANK]
                    V.tensor_tensor(half, half, prod[:, h, :], ALU.add).then_inc(s["brP_ready"], 1)
            def diagonal(f):
                V.tensor_tensor(diag, ident.unsqueeze(1).broadcast_to([P, DB, P]), over(fac[:, f, :], P), ALU.mult)\
                    .then_inc(s["diag_ready"], 1)

            def spread_read(n, bank):
                dve.wait_ge(s["spread_done"], n)
                ins = V.tensor_copy(spread[:, :].rearrange("p (h n) -> p h n", h=2), ps[:, bank:bank + 2, :])
                ins.then_inc(s["spread_ready"], 1)

            split_lo(34, 35, 36)
            mod_cols(1, 0)
            factor(1, 2 * DB, "post1_g", 0.0).then_inc(s["mod_ready"], 1)
            dve.wait_ge(s["m_turned"], 1)
            for n in range(4):
                act_lo_from(6 + n, ps[:, 4 + n, :].rearrange("p (b t) -> p b t", t=SEQ), 2 * n, 2 * n + 2)
            split_lo(37)
            dve.wait_ge(s["mod_ready"], 2)
            diagonal(1)
            split_lo(38)
            spread_read(1, 6)
            split_lo(39)
            V.tensor_copy(diag, over(mod[:, 3 * DB:4 * DB], P)).then_inc(s["shift_ready"], 1)
            mod_cols(2, 5)
            link(factor(2, 4 * DB, "pre2_g", 1.0))
            link(factor(3, 5 * DB, "post2_g", 0.0))
            split_lo(40)
            dve.wait_ge(s["logit0_done"], 1)
            V.tensor_copy(logit0[:, :], ps[:, 4, 0:EXPERTS]).then_inc(s["logit0_ready"], 1)
            split_lo(41)
            dve.wait_ge(s["logit0_ready"], 1)
            link(V.tensor_tensor(rw_sb[:, :, :], rw_sb[:, :, :], over(fac[:, 2, :], EXPERTS), ALU.mult))
            diagonal(3)
            y_ps = ps[:, 0:4, :].rearrange("p (t h) n -> p t (h n)", t=TT)
            dve.wait_ge(s["spread_ready"], 1)
            used(dve, "w_out", 3)
            V.tensor_tensor(yspread[:, 1, :], y_ps[:, 1, :], spread[:, :], ALU.mult).then_inc(s["y1_spread"], 1)
            dve.wait_ge(s["y0_squared"], 1)
            link(V.tensor_tensor(yspread[:, 0, :], y_ps[:, 0, :], spread[:, :], ALU.mult))
            variance(2, 2)
            rstd(2, 2, done=False)
            dve.wait_ge(s["y1_spread"], 1)
            for t in range(TT):
                V.scalar_tensor_tensor(out=x_sb[:, t, :], in0=yspread[:, t, :], scalar=stat[:, 2 + t:3 + t],
                                       in1=x_sb[:, t, :], op0=ALU.mult, op1=ALU.add).then_inc(s["x1_ready"], 1)
            dve.wait_ge(s["x1_ready"], TT)
            dve.wait_ge(s["x2_turned"], 1)
            V.tensor_copy(h2T[:, :, 0:P], x2T_ps[:, 0]).then_inc(s["h2_ready"], 1)
            variance(3, 4)
            rstd(3, 4, done=False)
            dve.wait_ge(s["logit_done"], 1)
            for t in range(TT):
                V.scalar_tensor_tensor(out=logit[:, t, :], in0=ps[:, 5, t * EXPERTS:(t + 1) * EXPERTS],
                                       scalar=stat[:, 4 + t:5 + t], in1=logit0[:, :], op0=ALU.mult, op1=ALU.add)\
                    .then_inc(s["logits_here"], 1)
            for t in range(TT):
                dve.wait_ge(s["logits_here"], t + 1)
                V.max(top_v[:, t, :], logit[:, t, :]).then_inc(s["max_here"], 1)
            for t in range(TT):
                dve.wait_ge(s["max_here"], t + 1)
                last = V.max_index(top_i[:, t, :], top_v[:, t, :], logit[:, t, :])
            link(last)
            link(V.tensor_copy(top_g[:, :, :], top_i[:, :, 0:TOP_K]))
            for t in range(TT):
                last = V.tensor_tensor(hot[:, t], k("expert").unsqueeze(1).broadcast_to([P, TOP_K, EXPERTS]),
                                       over(top_g[:, t, :], EXPERTS), ALU.is_equal)
            link(last)
            for t in range(TT):
                last = V.tensor_reduce(mask[:, t, :], hot[:, t].rearrange("p r e -> p e r"), AX.X, ALU.add)
            last.then_inc(s["mask_ready"], 1)
            for t in range(TT):
                last = V.tensor_scalar(top_f[:, t, :], top_v[:, t, 0:TOP_K], top_v[:, t, 0:1], None, ALU.subtract)
            last.then_inc(s["logit_ready"], 1)
            dve.wait_ge(s["count_done"], 1)
            V.tensor_scalar(nchunk[:, 1:CHUNKS], k("passed")[0:EXPERTS, :], ps[0:EXPERTS, 4, 0:1], 1.0, ALU.is_lt,
                            ALU.add, accum_out=nchunk[:, 0:1]).then_inc(s["nchunk_ready"], 1)
            dve.wait_ge(s["rank_done"], 1)
            dve.wait_ge(s["mask_ready"], 1)
            V.scalar_tensor_tensor(out=rank[:, :, :], in0=ps[:, 3, 0:TT * EXPERTS]
                                   .rearrange("p (t e) -> p t e", t=TT), scalar=1.0, in1=mask[:, :, :],
                                   op0=ALU.add, op1=ALU.mult).then_inc(s["rank_ready"], 1)
            dve.wait_ge(s["base_done"], 1)
            V.tensor_copy(base[:, 0:2 * EXPERTS + 1], ps[0:1, 5, 0:2 * EXPERTS + 1]).then_inc(s["base_ready"], 1)
            V.tensor_scalar(base[:, 2 * EXPERTS + 1:3 * EXPERTS + 1], ps[0:1, 5, 1:EXPERTS + 1], -1.0, None, ALU.add)\
                .then_inc(s["base_ready"], 1)
            dve.wait_ge(s["rank_ready"], 1)
            dve.wait_ge(s["base_ready"], 2)

            def picks(g, e, c):
                ge(dve, m["pick_turned"], g)
                for t in range(TT):
                    last = V.tensor_scalar(pick[:, t, :], slot[:, bass.ds(c, 1), 0:CAP]
                                           .rearrange("p o s -> p (o s)"), rank[:, t, bass.ds(e, 1)],
                                           stat[:, 4 + t:5 + t], ALU.is_equal, ALU.mult)
                    if t == 0:
                        V.tensor_copy(esel, k("row_of")[0:3 * EXPERTS, bass.ds(e, 1)]
                                      .broadcast_to([3 * EXPERTS, CAP]))
                last.then_inc(m["pick_ready"], 1)

            def gated_picks(e, c):
                for t in range(TT):
                    last = V.tensor_scalar(pickg[:, t, :], slot[:, bass.ds(c, 1), :].rearrange("p o s -> p (o s)"),
                                           rank[:, t, bass.ds(e, 1)], gate[:, t, bass.ds(e, 1)],
                                           ALU.is_equal, ALU.mult)
                last.then_inc(m["pickg_ready"], 1)

            def activate(g):
                dve.wait_ge(m["gu_done"], g)
                V.tensor_scalar(g_min, ps[:, GATE, :], LIMIT, None, ALU.min).then_inc(m["gmin_ready"], 1)
                V.tensor_scalar(u_clip, ps[:, UP, :], LIMIT, -LIMIT, ALU.min, ALU.max).then_inc(m["u_ready"], 1)
                dve.wait_ge(m["sig_ready"], g)
                V.tensor_tensor(g_act, g_min, g_sig, ALU.mult).then_inc(m["gact_ready"], 1)
                dve.wait_ge(m["gact_ready"], g)
                dve.wait_ge(m["u_ready"], g)
                V.scalar_tensor_tensor(out=act_sb, in0=u_clip, scalar=1.0, in1=g_act, op0=ALU.add, op1=ALU.mult)\
                    .then_inc(m["act_ready"], 1)

            def affine_gathered(g):
                dve.wait_ge(m["gathered"], g + 1)
                V.tensor_tensor(xg_m, ps[:, GATHER, :].rearrange("p (b s) -> p b s", s=CAP),
                                over(fac[:, 2, :], CAP), ALU.mult).then_inc(m["xgm_ready"], 1)
                dve.wait_ge(m["xgm_ready"], g + 1)
                V.tensor_tensor(xg, xg_m, over(mod[:, 3 * DB:4 * DB], CAP), ALU.add).then_inc(m["xg_ready"], 1)

            def accumulate(g):
                dve.wait_ge(m["scattered"], g)
                dve.wait_ge(m["acc_ready"], g)
                V.tensor_tensor(yacc[:, :, :], yacc[:, :, :],
                                ps[:, TURN:8, :].rearrange("p (t h) n -> p t (h n)", t=TT), ALU.add)\
                    .then_inc(m["acc_ready"], 1)

            def more_chunks(e):
                b0 = dve.value_load(base[0:1, bass.ds(e, 1)], min_val=0, max_val=MAX_CHUNKS)
                n = dve.value_load(base[0:1, bass.ds(e + EXPERTS + 1, 1)], min_val=1, max_val=CHUNKS)
                with dve.If(n > 1):
                    with dve.Fori(1, n) as c:
                        picks(b0 + c, e, c)
                        gated_picks(e, c)
                        activate(b0 + c)
                        affine_gathered(b0 + c)
                        accumulate(b0 + c)

            picks(0, 0, 0)
            dve.wait_ge(s["exp_ready"], 1)
            for t in range(TT):
                last = V.tensor_reduce(stat[:, 8 + t:9 + t], top_e[:, t, :], AX.X, ALU.add)
            link(last)
            link(V.reciprocal(stat[:, 8:8 + TT], stat[:, 8:8 + TT]))
            for t in range(TT):
                last = V.tensor_scalar(top_e[:, t, :], top_e[:, t, :], stat[:, 8 + t:9 + t], None, ALU.mult)
            link(last)
            for t in range(TT):
                last = V.tensor_tensor(hotg[:, t], hot[:, t], over(top_e[:, t, :], EXPERTS), ALU.mult)
            link(last)
            for t in range(TT):
                last = V.tensor_reduce(gate[:, t, :], hotg[:, t].rearrange("p r e -> p e r"), AX.X, ALU.add)
            last.then_inc(s["gate_ready"], 1)
            dve.wait_ge(s["gate_ready"], 1)
            gated_picks(0, 0)
            affine_gathered(0)
            more_chunks(0)
            with dve.Fori(1, EXPERTS) as e:
                b0 = dve.value_load(base[0:1, bass.ds(e, 1)], min_val=1, max_val=MAX_CHUNKS)
                picks(b0, e, 0)
                gated_picks(e, 0)
                activate(b0)
                affine_gathered(b0)
                accumulate(b0)
                more_chunks(e)
            n = dve.value_load(base[0:1, EXPERTS:EXPERTS + 1], min_val=EXPERTS, max_val=MAX_CHUNKS)
            activate(n)
            dve.wait_ge(m["acc_ready"], n)
            for t in range(TT):
                if t == 0:
                    dve.wait_ge(s["half_scattered"], 1)
                else:
                    dve.wait_ge(m["scattered"], n)
                V.tensor_tensor(yacc[:, t, :], yacc[:, t, :],
                                ps[:, TURN + 2 * t:TURN + 2 * t + 2, :].rearrange("p h n -> p (h n)"), ALU.add)\
                    .then_inc(s["ysum_ready"], 1)
            variance(4, 6, width=1)
            dve.wait_ge(s["spread_ready"], 2)
            dve.wait_ge(s["ysum_ready"], TT)
            V.tensor_tensor(yspread[:, 1, :], yacc[:, 1, :], spread[:, :], ALU.mult).then_inc(s["y1_spread"], 1)
            variance(5, 7, width=1)
            rstd(4, 6, done=False, width=1)

            def write_out(t):
                V.scalar_tensor_tensor(out=tail[:, t, :], in0=yspread[:, t, :], scalar=stat[:, 6 + t:7 + t],
                                       in1=x_sb[:, t, :], op0=ALU.mult, op1=ALU.add).then_inc(s["out_done"], 1)

            dve.wait_ge(s["y0_spread"], 1)
            write_out(0)
            rstd(5, 7, done=False, width=1)
            dve.wait_ge(s["y1_spread"], 2)
            write_out(1)


_INS = ["x", "c", "ada_w", "ada_b", "pre1_g", "post1_g", "pre2_g", "post2_g", "w_in", "pool_w", "pool_b",
        "pool_scale", "w_br_attn", "w_br_pool", "w_out", "router_w", "router_b", "w_gu", "b_gu", "w_dn", "b_dn"]


def constants(np):
    v = np.zeros((P, CONST_W), np.float32)
    row, colm = np.arange(P)[:, None], np.arange(P)[None, :]

    def put(name, value):
        a, b = CONSTS[name]
        v[:, a:b] = value

    put("ident", row == colm)
    put("tri_neg", np.where(row >= colm, -1.0, 0.0))
    put("ones_neg", -1.0)
    put("before", row < colm)
    put("ones", 1.0)
    tok, query = np.arange(SEQ)[:, None], np.arange(SEQ)[None, :]
    bands = []
    for w in WINDOWS:
        inside = (query - tok >= 0) & (query - tok < w)
        bands.append(np.where(inside, 1.0 / np.minimum(query + 1, w), 0.0) - (query == tok))
    put("band0", np.concatenate([b[0:P] for b in bands], axis=1))
    put("band1", np.concatenate([b[P:SEQ, P:SEQ] for b in bands], axis=1))
    put("slot", np.concatenate([CAP * n + 1 + np.arange(P) % CAP for n in range(CHUNKS)])[None, :])
    put("passed", CAP * np.arange(1, CHUNKS)[None, :])
    put("expert", np.arange(EXPERTS)[None, :])
    put("row_of", row % EXPERTS == np.arange(EXPERTS)[None, :])
    put("before_e", row < np.arange(EXPERTS + 1)[None, :])
    put("quad", row == 32 * np.arange(4)[None, :])
    return v


def kernel(**inputs):
    import numpy as np
    import concourse.bacc as bacc
    from concourse.bass_utils import run_bass_kernel_spmd

    nc = bacc.Bacc("TRN2", target_bir_lowering=False, num_devices=1)
    arrays, args = {}, []
    for name in _INS:
        a = np.ascontiguousarray(inputs[name])
        arrays[f"in_{name}"] = a
        args.append(nc.dram_tensor(f"in_{name}", a.shape, mybir.dt.from_np(a.dtype), kind="ExternalInput").ap())
    table = constants(np)
    arrays["in_consts"] = table
    args.append(nc.dram_tensor("in_consts", table.shape, mybir.dt.float32, kind="ExternalInput").ap())
    args.append(nc.dram_tensor("out_0", (1, SEQ, D), mybir.dt.float32, kind="ExternalOutput").ap())
    build(nc, *args)
    r = run_bass_kernel_spmd(nc, [arrays], core_ids=[0])
    return r.results[0]["out_0"]
```
